# Optimizing a Trainium2 kernel written in Bass

```python
import math
import jax, jax.numpy as jnp
from jax import lax
import numpy as np

D_MODEL = 1024
BATCH = 1
SEQ = 256
DEPTH = 2

MLA_HEADS = 6
MLA_Q_RANK = 384
MLA_KV_RANK = 256
MLA_NOPE = 64
MLA_ROPE = 32
MLA_QK = MLA_NOPE + MLA_ROPE
MLA_V = 64
DIFF_HEADS = 4
DIFF_QK = 64
DIFF_V = 2 * DIFF_QK
GQA_HEADS = 6
GQA_KV_HEADS = 2
GQA_GROUP = GQA_HEADS // GQA_KV_HEADS
GQA_DIM = 64
GRID_W = 64
Q_BLOCK = 128
ROPE_THETA = 10000.0
EPS = 1e-6
FFN_HIDDEN = -(-(8 * D_MODEL) // (3 * 256)) * 256

IN_SIZES = [
    MLA_Q_RANK, MLA_KV_RANK, MLA_ROPE,
    DIFF_HEADS * 2 * DIFF_QK, DIFF_HEADS * 2 * DIFF_QK, DIFF_HEADS * DIFF_V,
    GQA_HEADS * GQA_DIM, GQA_KV_HEADS * GQA_DIM, GQA_KV_HEADS * GQA_DIM,
]
IN_WIDTH = sum(IN_SIZES)
IN_OFFSETS = [int(v) for v in np.cumsum(IN_SIZES)[:-1]]
MIX_WIDTH = MLA_HEADS * MLA_V + DIFF_HEADS * DIFF_V + GQA_HEADS * GQA_DIM


def _rms_norm(x, gain):
    xf = x.astype(jnp.float32)
    y = xf * lax.rsqrt(jnp.mean(xf * xf, axis=-1, keepdims=True) + EPS)
    return (y * gain.astype(jnp.float32)).astype(x.dtype)

def _rope_cos_sin(pos, dim):
    inv = 1.0 / (ROPE_THETA ** (jnp.arange(0, dim, 2, dtype=jnp.float32) / dim))
    ang = pos.astype(jnp.float32)[:, None] * inv[None, :]
    return jnp.cos(ang), jnp.sin(ang)

def _apply_rope(x, cos, sin):
    xf = x.astype(jnp.float32)
    half = x.shape[-1] // 2
    x1, x2 = xf[..., :half], xf[..., half:]
    return jnp.concatenate([x1 * cos - x2 * sin, x1 * sin + x2 * cos], axis=-1).astype(x.dtype)

def _sweep_query_blocks(block_fn, q):
    s_len = q.shape[-2]
    nb = s_len // Q_BLOCK
    qb = q.reshape(q.shape[:-2] + (nb, Q_BLOCK, q.shape[-1]))
    qb = jnp.moveaxis(qb, -3, 0)
    out = lax.map(block_fn, qb)
    out = jnp.moveaxis(out, 0, -3)
    return out.reshape(out.shape[:-3] + (s_len, out.shape[-1]))

def _dense_attention(q, k, v, scale, score_eq, out_eq):
    def block_fn(qb):
        s = jnp.einsum(score_eq, qb, k).astype(jnp.float32) * scale
        p = jax.nn.softmax(s, axis=-1)
        return jnp.einsum(out_eq, p.astype(v.dtype), v)
    return _sweep_query_blocks(block_fn, q)

def _normal(key, shape, scale):
    return jax.random.normal(key, shape, jnp.float32) * scale

def _gain(key, shape):
    return 1.0 + 0.02 * jax.random.normal(key, shape, jnp.float32)

def first_inputs(seed: int = 0) -> dict:
    key = jax.random.key(seed)
    ks = jax.random.split(key, 24)
    L = DEPTH
    return {
        "x": jax.random.normal(ks[0], (BATCH, SEQ, D_MODEL), jnp.float32),
        "attn_norm": _gain(ks[1], (L, D_MODEL)),
        "w_in": _normal(ks[2], (L, D_MODEL, IN_WIDTH), D_MODEL ** -0.5),
        "mla_q_norm": _gain(ks[3], (L, MLA_Q_RANK)),
        "mla_w_uq": _normal(ks[4], (L, MLA_Q_RANK, MLA_HEADS * MLA_QK), MLA_Q_RANK ** -0.5),
        "mla_kv_norm": _gain(ks[5], (L, MLA_KV_RANK)),
        "mla_w_ukv": _normal(ks[6], (L, MLA_KV_RANK, MLA_HEADS * (MLA_NOPE + MLA_V)), MLA_KV_RANK ** -0.5),
        "mla_q_gain": _gain(ks[7], (L, MLA_QK)),
        "mla_k_gain": _gain(ks[8], (L, MLA_QK)),
        "diff_q_gain": _gain(ks[9], (L, DIFF_QK)),
        "diff_k_gain": _gain(ks[10], (L, DIFF_QK)),
        "diff_lq1": _normal(ks[11], (L, DIFF_QK), 0.1),
        "diff_lk1": _normal(ks[12], (L, DIFF_QK), 0.1),
        "diff_lq2": _normal(ks[13], (L, DIFF_QK), 0.1),
        "diff_lk2": _normal(ks[14], (L, DIFF_QK), 0.1),
        "diff_out_gain": _gain(ks[15], (L, DIFF_V)),
        "gqa_q_gain": _gain(ks[16], (L, GQA_DIM)),
        "gqa_k_gain": _gain(ks[17], (L, GQA_DIM)),
        "w_o": _normal(ks[18], (L, MIX_WIDTH, D_MODEL), MIX_WIDTH ** -0.5),
        "ffn_norm": _gain(ks[19], (L, D_MODEL)),
        "w_gate_up": _normal(ks[20], (L, D_MODEL, 2 * FFN_HIDDEN), D_MODEL ** -0.5),
        "w_down": _normal(ks[21], (L, FFN_HIDDEN, D_MODEL), FFN_HIDDEN ** -0.5),
    }

def first_block(x, attn_norm, w_in, mla_q_norm, mla_w_uq, mla_kv_norm, mla_w_ukv,
              mla_q_gain, mla_k_gain, diff_q_gain, diff_k_gain, diff_lq1, diff_lk1,
              diff_lq2, diff_lk2, diff_out_gain, gqa_q_gain, gqa_k_gain, w_o,
              ffn_norm, w_gate_up, w_down):
    B, S, _ = x.shape
    rows = S // GRID_W
    pos = jnp.arange(S, dtype=jnp.int32)
    cos_mla, sin_mla = _rope_cos_sin(pos, MLA_ROPE)
    cos_dif, sin_dif = _rope_cos_sin(pos, DIFF_QK)
    row_idx, col_idx = jnp.meshgrid(jnp.arange(rows, dtype=jnp.int32),
                                    jnp.arange(GRID_W, dtype=jnp.int32), indexing="ij")
    half_ax = GQA_DIM // 2
    cos_row, sin_row = _rope_cos_sin(row_idx.reshape(-1), half_ax)
    cos_col, sin_col = _rope_cos_sin(col_idx.reshape(-1), half_ax)

    def axial_rope(t):
        return jnp.concatenate([_apply_rope(t[..., :half_ax], cos_row, sin_row),
                                _apply_rope(t[..., half_ax:], cos_col, sin_col)], axis=-1)

    for l in range(DEPTH):
        xn = _rms_norm(x, attn_norm[l])
        h = xn @ w_in[l]
        (h_cq, h_ckv, h_kr, h_dq, h_dk, h_dv, h_gq, h_gk, h_gv) = jnp.split(h, IN_OFFSETS, axis=-1)

        c_q = _rms_norm(h_cq, mla_q_norm[l])
        q_a = (c_q @ mla_w_uq[l]).reshape(B, S, MLA_HEADS, MLA_QK).transpose(0, 2, 1, 3)
        c_kv = _rms_norm(h_ckv, mla_kv_norm[l])
        kv_a = (c_kv @ mla_w_ukv[l]).reshape(B, S, MLA_HEADS, MLA_NOPE + MLA_V).transpose(0, 2, 1, 3)
        k_nope, v_a = kv_a[..., :MLA_NOPE], kv_a[..., MLA_NOPE:]
        k_rope = jnp.broadcast_to(h_kr[:, None, :, :], (B, MLA_HEADS, S, MLA_ROPE))
        k_a = jnp.concatenate([k_nope, k_rope], axis=-1)
        q_a = _rms_norm(q_a, mla_q_gain[l])
        k_a = _rms_norm(k_a, mla_k_gain[l])
        q_a = jnp.concatenate([q_a[..., :MLA_NOPE], _apply_rope(q_a[..., MLA_NOPE:], cos_mla, sin_mla)], axis=-1)
        k_a = jnp.concatenate([k_a[..., :MLA_NOPE], _apply_rope(k_a[..., MLA_NOPE:], cos_mla, sin_mla)], axis=-1)
        o_a = _dense_attention(q_a, k_a, v_a, MLA_QK ** -0.5,
                               "bhqd,bhsd->bhqs", "bhqs,bhsv->bhqv")
        o_a = o_a.transpose(0, 2, 1, 3).reshape(B, S, MLA_HEADS * MLA_V)

        q_b = h_dq.reshape(B, S, DIFF_HEADS, 2, DIFF_QK).transpose(0, 2, 3, 1, 4)
        k_b = h_dk.reshape(B, S, DIFF_HEADS, 2, DIFF_QK).transpose(0, 2, 3, 1, 4)
        v_b = h_dv.reshape(B, S, DIFF_HEADS, DIFF_V).transpose(0, 2, 1, 3)
        q_b = _apply_rope(_rms_norm(q_b, diff_q_gain[l]), cos_dif, sin_dif)
        k_b = _apply_rope(_rms_norm(k_b, diff_k_gain[l]), cos_dif, sin_dif)
        lambda_init = 0.8 - 0.6 * math.exp(-0.3 * l)
        lam = (jnp.exp(jnp.sum(diff_lq1[l].astype(jnp.float32) * diff_lk1[l].astype(jnp.float32)))
               - jnp.exp(jnp.sum(diff_lq2[l].astype(jnp.float32) * diff_lk2[l].astype(jnp.float32)))
               + lambda_init)
        scale_b = DIFF_QK ** -0.5

        def diff_block(qb, k_b=k_b, v_b=v_b, lam=lam):
            s = jnp.einsum("bhcqd,bhcsd->bhcqs", qb, k_b).astype(jnp.float32) * scale_b
            p = jax.nn.softmax(s, axis=-1)
            a = p[:, :, 0] - lam * p[:, :, 1]
            return jnp.einsum("bhqs,bhsv->bhqv", a.astype(v_b.dtype), v_b)

        o_b = _sweep_query_blocks(diff_block, q_b)
        o_b = (_rms_norm(o_b, diff_out_gain[l]) * (1.0 - lambda_init)).astype(x.dtype)
        o_b = o_b.transpose(0, 2, 1, 3).reshape(B, S, DIFF_HEADS * DIFF_V)

        q_c = h_gq.reshape(B, S, GQA_KV_HEADS, GQA_GROUP, GQA_DIM).transpose(0, 2, 3, 1, 4)
        k_c = h_gk.reshape(B, S, GQA_KV_HEADS, GQA_DIM).transpose(0, 2, 1, 3)
        v_c = h_gv.reshape(B, S, GQA_KV_HEADS, GQA_DIM).transpose(0, 2, 1, 3)
        q_c = axial_rope(_rms_norm(q_c, gqa_q_gain[l]))
        k_c = axial_rope(_rms_norm(k_c, gqa_k_gain[l]))
        o_c = _dense_attention(q_c, k_c, v_c, GQA_DIM ** -0.5,
                               "bkgqd,bksd->bkgqs", "bkgqs,bksv->bkgqv")
        o_c = o_c.transpose(0, 3, 1, 2, 4).reshape(B, S, GQA_HEADS * GQA_DIM)

        mix = jnp.concatenate([o_a, o_b, o_c], axis=-1)
        x = x + mix @ w_o[l]

        xn = _rms_norm(x, ffn_norm[l])
        gate, up = jnp.split(xn @ w_gate_up[l], 2, axis=-1)
        x = x + (jax.nn.silu(gate) * up) @ w_down[l]
    return x


HEAD_DIM = 64
NA_HEADS = 8
NA_WIDTH = NA_HEADS * HEAD_DIM
NA_KH_MAX = 8
NA_KW = 16
NA_QCOLS = 16
NA_KCOLS = NA_QCOLS + NA_KW
SW_HEADS = 8
SW_KV_HEADS = 2
SW_GROUP = SW_HEADS // SW_KV_HEADS
SW_WIDTH = SW_HEADS * HEAD_DIM
SW_KV_WIDTH = SW_KV_HEADS * HEAD_DIM
SW_WINDOW = 128
SW_BLOCK = 128
ROT_DIM = HEAD_DIM // 4
ROPE_THETA_2 = 500000.0
OFF_QNA = NA_WIDTH
OFF_KNA = 2 * NA_WIDTH
OFF_VNA = 3 * NA_WIDTH
OFF_QSW = OFF_VNA + SW_WIDTH
OFF_KSW = OFF_QSW + SW_KV_WIDTH
OFF_VSW = OFF_KSW + SW_KV_WIDTH
N_BRANCHES = 2
PROJ_COLS = OFF_VSW + N_BRANCHES * D_MODEL
D_FF_DENSE = 2816
N_EXPERTS = 8
TOP_K = 2
D_FF_EXPERT = 3584
N_DENSE_LAYERS = (DEPTH + 1) // 2
N_MOE_LAYERS = DEPTH // 2
DEEPNORM_ALPHA = (2 * DEPTH) ** 0.25
DEEPNORM_BETA = (8 * DEPTH) ** -0.25
LN_EPS = 1e-5
NEG_INF = -1e30


def layer_norm(x, g, b):
    xf = x.astype(jnp.float32)
    mu = jnp.mean(xf, axis=-1, keepdims=True)
    var = jnp.mean(jnp.square(xf - mu), axis=-1, keepdims=True)
    return ((xf - mu) * lax.rsqrt(var + LN_EPS)).astype(x.dtype) * g + b

def partial_rotary(x, pos):
    half = ROT_DIM // 2
    inv_freq = 1.0 / (ROPE_THETA_2 ** (jnp.arange(0, ROT_DIM, 2, dtype=jnp.float32) / ROT_DIM))
    ang = pos.astype(jnp.float32)[:, None] * inv_freq[None, :]
    cos = jnp.cos(ang)[None, :, None, :]
    sin = jnp.sin(ang)[None, :, None, :]
    x1 = x[..., :half].astype(jnp.float32)
    x2 = x[..., half:ROT_DIM].astype(jnp.float32)
    rot = jnp.concatenate([x1 * cos - x2 * sin, x2 * cos + x1 * sin], axis=-1).astype(x.dtype)
    return jnp.concatenate([rot, x[..., ROT_DIM:]], axis=-1)

def neighbourhood_attention(q, k, v, rpb):
    B, S, H, D = q.shape
    rows = S // GRID_W
    kh = min(NA_KH_MAX, rows)
    n_cb = GRID_W // NA_QCOLS
    r = np.arange(rows)
    row_start = np.clip(r - kh // 2, 0, rows - kh)
    key_rows = row_start[:, None] + np.arange(kh)[None, :]
    cb_start = np.clip(np.arange(n_cb) * NA_QCOLS - NA_KW // 2, 0, GRID_W - NA_KCOLS)
    key_cols = cb_start[:, None] + np.arange(NA_KCOLS)[None, :]
    key_tok = (key_rows[:, None, :, None] * GRID_W + key_cols[None, :, None, :])
    key_tok = key_tok.reshape(rows, n_cb, kh * NA_KCOLS)
    kg = jnp.take(k, key_tok, axis=1)
    vg = jnp.take(v, key_tok, axis=1)
    qb = q.reshape(B, rows, n_cb, NA_QCOLS, H, D)
    s = jnp.einsum('brjqhd,brjkhd->brjhqk', qb, kg,
                   preferred_element_type=jnp.float32) * (D ** -0.5)
    qcol = np.arange(n_cb)[:, None] * NA_QCOLS + np.arange(NA_QCOLS)[None, :]
    qcs = np.clip(qcol - NA_KW // 2, 0, GRID_W - NA_KW)
    kcol = key_cols[:, None, :]
    valid = (kcol >= qcs[..., None]) & (kcol < qcs[..., None] + NA_KW)
    dr = key_rows - r[:, None] + (NA_KH_MAX - 1)
    dc = np.clip(kcol - qcol[..., None] + (NA_KW - 1), 0, 2 * NA_KW - 2)
    dri = dr[:, None, None, :, None]
    dci = dc[None, :, :, None, :]
    bias = rpb[:, dri, dci].astype(jnp.float32)
    mask = np.broadcast_to(valid[None, :, :, None, :], (rows, n_cb, NA_QCOLS, kh, NA_KCOLS))
    bias = jnp.where(mask[None], bias, NEG_INF)
    bias = bias.reshape(H, rows, n_cb, NA_QCOLS, kh * NA_KCOLS).transpose(1, 2, 0, 3, 4)
    p = jax.nn.softmax(s + bias[None], axis=-1)
    o = jnp.einsum('brjhqk,brjkhd->brjqhd', p.astype(v.dtype), vg)
    return o.reshape(B, S, H * D)

def sliding_window_attention(q, k, v, sink):
    B, S, HQ, D = q.shape
    nb = S // SW_BLOCK
    pad = ((0, 0), (SW_BLOCK, SW_BLOCK), (0, 0), (0, 0))
    kp = jnp.pad(k, pad).reshape(B, nb + 2, SW_BLOCK, SW_KV_HEADS, D)
    vp = jnp.pad(v, pad).reshape(B, nb + 2, SW_BLOCK, SW_KV_HEADS, D)
    kb = jnp.concatenate([kp[:, :-2], kp[:, 1:-1], kp[:, 2:]], axis=2)
    vb = jnp.concatenate([vp[:, :-2], vp[:, 1:-1], vp[:, 2:]], axis=2)
    qb = q.reshape(B, nb, SW_BLOCK, SW_KV_HEADS, SW_GROUP, D)
    s = jnp.einsum('bnqkgd,bnskd->bnkgqs', qb, kb,
                   preferred_element_type=jnp.float32) * (D ** -0.5)
    qpos = np.arange(SW_BLOCK)[:, None] + SW_BLOCK
    kpos = np.arange(3 * SW_BLOCK)[None, :]
    band = np.abs(qpos - kpos) <= SW_WINDOW
    kabs = np.arange(nb)[:, None, None] * SW_BLOCK + kpos[None] - SW_BLOCK
    valid = band[None] & (kabs >= 0) & (kabs < S)
    s = jnp.where(valid[None, :, None, None], s, NEG_INF)
    sink_logit = sink.astype(jnp.float32).reshape(SW_KV_HEADS, SW_GROUP)[None, None, :, :, None, None]
    m = jnp.maximum(jnp.max(s, axis=-1, keepdims=True), sink_logit)
    p = jnp.exp(s - m)
    denom = jnp.sum(p, axis=-1, keepdims=True) + jnp.exp(sink_logit - m)
    o = jnp.einsum('bnkgqs,bnskd->bnqkgd', (p / denom).astype(v.dtype), vb)
    return o.reshape(B, S, HQ * D)

def mixer_block(x, w_in, b_gate, rpb, sink, w_branch_na, w_branch_sw, w_out):
    B, S, _ = x.shape
    proj = x @ w_in
    q_na, k_na, v_na, q_sw, k_sw, v_sw, gate_logits = jnp.split(
        proj, [OFF_QNA, OFF_KNA, OFF_VNA, OFF_QSW, OFF_KSW, OFF_VSW], axis=-1)
    hs = lambda t, h: t.reshape(B, S, h, HEAD_DIM)
    y_na = neighbourhood_attention(hs(q_na, NA_HEADS), hs(k_na, NA_HEADS), hs(v_na, NA_HEADS), rpb)
    pos = jnp.arange(S, dtype=jnp.int32)
    qs = partial_rotary(hs(q_sw, SW_HEADS), pos)
    ks = partial_rotary(hs(k_sw, SW_KV_HEADS), pos)
    y_sw = sliding_window_attention(qs, ks, hs(v_sw, SW_KV_HEADS), sink)
    y_na = y_na @ w_branch_na
    y_sw = y_sw @ w_branch_sw
    gates = jax.nn.sigmoid((gate_logits + b_gate).astype(jnp.float32)).astype(x.dtype)
    g_na, g_sw = jnp.split(gates, N_BRANCHES, axis=-1)
    return (g_na * y_na + g_sw * y_sw) @ w_out

def swiglu(x, w_gate, w_up, w_down):
    return (jax.nn.silu(x @ w_gate) * (x @ w_up)) @ w_down

def moe_swiglu(x, w_router, w_gate, w_up, w_down):
    B, S, D = x.shape
    xt = x.reshape(B * S, D)
    logits = (xt @ w_router).astype(jnp.float32)
    top_vals, top_idx = lax.top_k(logits, TOP_K)
    top_w = jax.nn.softmax(top_vals, axis=-1)
    combine = jnp.sum(jax.nn.one_hot(top_idx, N_EXPERTS, dtype=jnp.float32) * top_w[..., None], axis=1)
    combine = combine.astype(x.dtype)
    y = jnp.zeros_like(xt)
    for e in range(N_EXPERTS):
        y = y + combine[:, e:e + 1] * swiglu(xt, w_gate[e], w_up[e], w_down[e])
    return y.reshape(B, S, D)

def second_inputs(seed: int = 0) -> dict:
    key = jax.random.key(seed)
    ks = jax.random.split(key, 24)
    f32 = jnp.float32
    nrm = lambda k, shape, scale: jax.random.normal(k, shape, f32) * scale
    beta = DEEPNORM_BETA
    col_scale = np.ones((PROJ_COLS,), np.float32)
    col_scale[OFF_KNA:OFF_VNA] = beta
    col_scale[OFF_KSW:OFF_VSW] = beta
    w_in = nrm(ks[1], (DEPTH, D_MODEL, PROJ_COLS), D_MODEL ** -0.5) * jnp.asarray(col_scale)
    return {
        "x": nrm(ks[0], (BATCH, SEQ, D_MODEL), 1.0),
        "emb_ln_g": 1.0 + nrm(ks[2], (D_MODEL,), 0.02),
        "emb_ln_b": nrm(ks[3], (D_MODEL,), 0.02),
        "w_in": w_in,
        "b_gate": nrm(ks[4], (DEPTH, N_BRANCHES * D_MODEL), 0.1),
        "na_rpb": nrm(ks[5], (DEPTH, NA_HEADS, 2 * NA_KH_MAX - 1, 2 * NA_KW - 1), 0.2),
        "sw_sink": nrm(ks[6], (DEPTH, SW_HEADS), 0.5),
        "w_branch_na": nrm(ks[7], (DEPTH, NA_WIDTH, D_MODEL), beta * NA_WIDTH ** -0.5),
        "w_branch_sw": nrm(ks[8], (DEPTH, SW_WIDTH, D_MODEL), beta * SW_WIDTH ** -0.5),
        "w_out": nrm(ks[9], (DEPTH, D_MODEL, D_MODEL), beta * D_MODEL ** -0.5),
        "ln1_g": 1.0 + nrm(ks[10], (DEPTH, D_MODEL), 0.02),
        "ln1_b": nrm(ks[11], (DEPTH, D_MODEL), 0.02),
        "ffn_w_gate": nrm(ks[12], (N_DENSE_LAYERS, D_MODEL, D_FF_DENSE), beta * D_MODEL ** -0.5),
        "ffn_w_up": nrm(ks[13], (N_DENSE_LAYERS, D_MODEL, D_FF_DENSE), beta * D_MODEL ** -0.5),
        "ffn_w_down": nrm(ks[14], (N_DENSE_LAYERS, D_FF_DENSE, D_MODEL), beta * D_FF_DENSE ** -0.5),
        "moe_router": nrm(ks[15], (N_MOE_LAYERS, D_MODEL, N_EXPERTS), D_MODEL ** -0.5),
        "moe_w_gate": nrm(ks[16], (N_MOE_LAYERS, N_EXPERTS, D_MODEL, D_FF_EXPERT), beta * D_MODEL ** -0.5),
        "moe_w_up": nrm(ks[17], (N_MOE_LAYERS, N_EXPERTS, D_MODEL, D_FF_EXPERT), beta * D_MODEL ** -0.5),
        "moe_w_down": nrm(ks[18], (N_MOE_LAYERS, N_EXPERTS, D_FF_EXPERT, D_MODEL), beta * D_FF_EXPERT ** -0.5),
        "ln2_g": 1.0 + nrm(ks[19], (DEPTH, D_MODEL), 0.02),
        "ln2_b": nrm(ks[20], (DEPTH, D_MODEL), 0.02),
    }

def second_block(x, emb_ln_g, emb_ln_b, w_in, b_gate, na_rpb, sw_sink, w_branch_na, w_branch_sw,
              w_out, ln1_g, ln1_b, ffn_w_gate, ffn_w_up, ffn_w_down, moe_router, moe_w_gate,
              moe_w_up, moe_w_down, ln2_g, ln2_b):
    x = layer_norm(x, emb_ln_g, emb_ln_b)
    for layer in range(DEPTH):
        m = mixer_block(x, w_in[layer], b_gate[layer], na_rpb[layer], sw_sink[layer],
                        w_branch_na[layer], w_branch_sw[layer], w_out[layer])
        x = layer_norm(DEEPNORM_ALPHA * x + m, ln1_g[layer], ln1_b[layer])
        i = layer // 2
        if layer % 2 == 0:
            f = swiglu(x, ffn_w_gate[i], ffn_w_up[i], ffn_w_down[i])
        else:
            f = moe_swiglu(x, moe_router[i], moe_w_gate[i], moe_w_up[i], moe_w_down[i])
        x = layer_norm(DEEPNORM_ALPHA * x + f, ln2_g[layer], ln2_b[layer])
    return x


def setup_inputs(seed=0):
    out = dict(first_inputs(seed))
    for name, value in second_inputs(seed + 1).items():
        if name != "x":
            out[name + "_2"] = value
    return out


def reference(
    x, attn_norm, w_in, mla_q_norm, mla_w_uq, mla_kv_norm, mla_w_ukv, mla_q_gain, mla_k_gain,
    diff_q_gain, diff_k_gain, diff_lq1, diff_lk1, diff_lq2, diff_lk2, diff_out_gain, gqa_q_gain,
    gqa_k_gain, w_o, ffn_norm, w_gate_up, w_down, emb_ln_g_2, emb_ln_b_2, w_in_2, b_gate_2,
    na_rpb_2, sw_sink_2, w_branch_na_2, w_branch_sw_2, w_out_2, ln1_g_2, ln1_b_2, ffn_w_gate_2,
    ffn_w_up_2, ffn_w_down_2, moe_router_2, moe_w_gate_2, moe_w_up_2, moe_w_down_2, ln2_g_2,
    ln2_b_2,
):
    x = first_block(
        x, attn_norm, w_in, mla_q_norm, mla_w_uq, mla_kv_norm, mla_w_ukv, mla_q_gain,
        mla_k_gain, diff_q_gain, diff_k_gain, diff_lq1, diff_lk1, diff_lq2, diff_lk2,
        diff_out_gain, gqa_q_gain, gqa_k_gain, w_o, ffn_norm, w_gate_up, w_down,
    )
    return second_block(
        x, emb_ln_g_2, emb_ln_b_2, w_in_2, b_gate_2, na_rpb_2, sw_sink_2, w_branch_na_2,
        w_branch_sw_2, w_out_2, ln1_g_2, ln1_b_2, ffn_w_gate_2, ffn_w_up_2, ffn_w_down_2,
        moe_router_2, moe_w_gate_2, moe_w_up_2, moe_w_down_2, ln2_g_2, ln2_b_2,
    )


_drawn_inputs = setup_inputs


def setup_inputs(seed=0):
    import zlib

    import numpy as np

    out = dict(_drawn_inputs(seed))
    spreads = {}
    factors = {'mla_q_norm': 8.0,
     'mla_kv_norm': 8.0,
     'mla_q_gain': 8.0,
     'mla_k_gain': 8.0,
     'diff_q_gain': 4.109,
     'diff_k_gain': 3.832,
     'diff_out_gain': 4.325,
     'gqa_q_gain': 8.0,
     'gqa_k_gain': 8.0,
     'ffn_norm': 3.022,
     'emb_ln_g_2': 7.748,
     'emb_ln_b_2': 7.743,
     'b_gate_2': 34.288,
     'na_rpb_2': 8.0,
     'sw_sink_2': 64.0}
    for name, (base, spread) in spreads.items():
        noise = np.random.default_rng([zlib.crc32(name.encode()), seed]).standard_normal(out[name].shape)
        drawn = base * np.exp(spread * noise) if base else spread * noise
        out[name] = __import__('jax').numpy.asarray(drawn.astype(out[name].dtype))
    for name, factor in factors.items():
        out[name] = (out[name] * factor).astype(out[name].dtype)
    return out
```

```python
import math
from contextlib import ExitStack

import numpy as np

import concourse.bass as bass
from concourse import mybir

F32 = mybir.dt.float32
F32R = mybir.dt.float32r
I32 = mybir.dt.int32
U32 = mybir.dt.uint32
ALU = mybir.AluOpType
ACT = mybir.ActivationFunctionType
AX = mybir.AxisListType

P = 128
S = 256
TB = S // P
D = 1024
KD = D // P
LAYERS = 2
EPS = 1e-6
SMALL = 680
LN_EPS = 1e-5
ALPHA = (2 * LAYERS) ** 0.25

MH, MQR, MKVR, MNOPE, MROPE, MV = 6, 384, 256, 64, 32, 64
MQK = MNOPE + MROPE
DH, DQ = 4, 64
DV = 2 * DQ
GH, GKV, GD = 6, 2, 64
C_CQ, C_CKV = 0, MQR
C_KR = C_CKV + MKVR
C_DQ = C_KR + MROPE
C_DK = C_DQ + 2 * DH * DQ
C_DV = C_DK + 2 * DH * DQ
C_GQ = C_DV + DH * DV
C_GK = C_GQ + GH * GD
C_GV = C_GK + GKV * GD
W_IN1 = C_GV + GKV * GD
MIX = MH * MV + DH * DV + GH * GD
FF1 = 2816

HD = 64
NH, SH, SKV = 8, 8, 2
W_NA = NH * HD
W_QKV2 = 3 * W_NA + SH * HD + 2 * SKV * HD
C_QS = 3 * W_NA
C_KS = C_QS + SH * HD
C_VS = C_KS + SKV * HD
ROT = HD // 4
GRID_W = 64
ROWS = S // GRID_W
NE = 8
FFE = 3584
NEG = -1e30

GROUP = 2048
HALF = GROUP // 2
RAW = 6
SPLIT = 4
AHEAD = SPLIT - 1
PERIOD = 2 * RAW
FC = 256


def chunks_in1():
    return [(c, min(512, W_IN1 - c)) for c in range(0, W_IN1, 512)]


def chunks_in2():
    return [(c, min(512, W_QKV2 - c)) for c in range(0, W_QKV2, 512)] + [
        (W_QKV2 + c, 512) for c in range(0, 2 * D, 512)]


def halves_of(width):
    return 2 if width == 256 else 4


H_IN1 = sum(halves_of(w) for _, w in chunks_in1())
H_UQ, H_UKV, H_O = MQR // P, MKVR // P, MIX // P
H_FF1 = FF1 // FC * 6
H_L1 = H_IN1 + H_UQ + H_UKV + H_O + H_FF1
H_MIX2 = sum(halves_of(w) for _, w in chunks_in2()) + 2 * (W_NA // P) + D // P
H_EXP = FFE // FC * 6
H_DENSE = LAYERS * H_L1 + 2 * H_MIX2 + H_FF1
MOE_AT = H_DENSE + (H_DENSE % 2)
TOTAL = MOE_AT + NE * H_EXP
assert H_EXP % PERIOD == 0 and MOE_AT % 2 == 0

A_H = 0
A_QA = A_H + TB * W_IN1
A_KV = A_QA + TB * MH * MQK
A_KA = A_KV + TB * MH * (MNOPE + MV)
A_QK = A_KA + TB * MH * MQK
N_QK1 = 2 * MH + 2 * DH + GH // GKV + 1
A_END = A_QK + N_QK1 * S
B_H = 0
B_G = B_H + TB * W_QKV2
B_QK = B_G + TB * 2 * D
N_QK2 = NH + SH // SKV + 1
N_MAP1 = 2 * DH + GH + MH
N_MAP2 = NH + SH
B_SS = B_QK + N_QK2 * S
B_BT = B_SS + 2 * TB * S
NBT = 3
B_T = B_BT + NBT * TB * S
E_SIL = 0
E_HH = E_SIL + TB * FC
E_S = E_HH + TB * FC
E_SW = E_S + TB * P
E_SWT = E_SW + TB * P
E_YE = E_SWT + S
E_ACC = E_YE + D
E_EQ = E_ACC + TB * D

ROPEW = 2 * (MQK + DQ + GD)
F_MQ, F_MK, F_DQ, F_DK, F_GQ, F_GK = 0, MQK, 2 * MQK, 2 * MQK + DQ, 2 * MQK + 2 * DQ, 2 * MQK + 2 * DQ + GD
R_G, R_GS, R_OG, R_LAM = 0, ROPEW, 2 * ROPEW, 2 * ROPEW + DV
ROWV = R_LAM + 4 * DQ
CG_ATTN, CG_FFN, CG_Q, CG_KV = 0, KD, 2 * KD, 2 * KD + MQR // P
CGW = CG_KV + MKVR // P


class Count:

    def __init__(self):
        self.base, self.n, self.saved = 0, 0, []

    def at(self, d=0):
        return self.base + (self.n + d)

    def enter(self, i, per):
        self.saved.append((self.base, self.n, per))
        self.base = self.base + (i * per + self.n)
        self.n = 0

    def leave(self, trips):
        base, n, per = self.saved.pop()
        assert self.n == per, (self.n, per)
        self.base, self.n = base, n + trips * per


def wait(e, sem, value):
    if not isinstance(value, int) or value > 0:
        e.wait_ge(sem, value)


class Stream:

    def __init__(self):
        self.s, self.periods = 0, 0

    def half(self, d=0):
        s = self.s + d
        return s, self.periods

    def done(self, d=0):
        return self.periods * PERIOD + (self.s + d + 1)


def build(nc, A):
    ctx = ExitStack()
    with ctx:
        def sb(name, shape, dt=F32):
            return ctx.enter_context(nc.sbuf_tensor(name, shape, dt))

        def sem(name):
            return ctx.enter_context(nc.semaphore(name))

        raw = sb("raw", [P, RAW, GROUP])
        w_hi = sb("w_hi", [P, SPLIT, HALF], F32R)
        w_lo = sb("w_lo", [P, SPLIT, HALF], F32R)
        X = sb("X", [P, TB, D])
        KX = MIX // P
        x_hi = sb("x_hi", [P, KX, S], F32R)
        x_lo = sb("x_lo", [P, KX, S], F32R)
        O = sb("O", [P, TB, MIX])
        arena = sb("arena", [P, max(A_END, B_T + 1024)])
        PP = sb("PP", [P, 2, TB, S])
        PT = sb("PT", [P, 2, TB, S])
        tab = sb("tab", [P, 2 * TB * ROPEW + ROWV])
        t3 = sb("t3", [P, TB * DV])
        small = sb("small", [P, SMALL])
        ident = sb("ident", [P, P])
        colg = sb("colg", [P, LAYERS, CGW])
        rw_hi = sb("rw_hi", [P, KD, NE], F32R)
        rw_lo = sb("rw_lo", [P, KD, NE], F32R)
        flag = sb("flag", [P, 8], I32)
        idx = sb("idx", [P, TB, 8], U32)
        bank = [ctx.enter_context(nc.psum_tensor(f"bank{i}", [P, 512], F32)) for i in range(8)]

        XS = O[:, :, 0:D]
        H = arena[:, A_H:A_QA].rearrange("p (t n) -> p t n", t=TB)
        QA = arena[:, A_QA:A_KV].rearrange("p (t n) -> p t n", t=TB)
        KV = arena[:, A_KV:A_KA].rearrange("p (t n) -> p t n", t=TB)
        KA = arena[:, A_KA:A_QK].rearrange("p (t n) -> p t n", t=TB)
        QK1 = arena[:, A_QK:A_END].rearrange("p (b n) -> p b n", n=S)
        H2 = arena[:, B_H:B_G].rearrange("p (t n) -> p t n", t=TB)
        G2 = arena[:, B_G:B_QK].rearrange("p (t n) -> p t n", t=TB)
        QK2 = arena[:, B_QK:B_SS].rearrange("p (b n) -> p b n", n=S)
        SS = arena[:, B_SS:B_BT].rearrange("p (b t n) -> p b t n", b=2, t=TB)
        BT = arena[:, B_BT:B_T].rearrange("p (b t n) -> p b t n", b=NBT, t=TB)
        T2 = arena[:, B_T:B_T + 1024]
        YG = arena[:, B_H:B_H + TB * D].rearrange("p (t n) -> p t n", t=TB)
        SIL = arena[:, E_SIL:E_HH].rearrange("p (t n) -> p t n", t=TB)
        HH = arena[:, E_HH:E_S].rearrange("p (t n) -> p t n", t=TB)
        SE = arena[:, E_S:E_SW].rearrange("p (t n) -> p t n", t=TB)
        SW = arena[:, E_SW:E_SWT].rearrange("p (t n) -> p t n", t=TB)
        SWT = arena[:, E_SWT:E_YE]
        YE = arena[:, E_YE:E_ACC]
        ACC = arena[:, E_ACC:E_EQ].rearrange("p (t n) -> p t n", t=TB)
        CT = tab[:, 0:TB * ROPEW].rearrange("p (t n) -> p t n", t=TB)
        ST = tab[:, TB * ROPEW:2 * TB * ROPEW].rearrange("p (t n) -> p t n", t=TB)
        rowv = tab[:, 2 * TB * ROPEW:]
        GB = tab[:, 0:2 * D]
        BG = PP[:, :, :, :].rearrange("p b t n -> p (b t n)")
        BG2 = PT[:, :, :, :].rearrange("p b t n -> p (b t n)")
        t1, t2 = BG, BG2
        hT_hi, hT_lo = x_hi[:, KD:KD + 2, :], x_lo[:, KD:KD + 2, :]

        at = [0]

        def sm(n):
            at[0] += n
            assert at[0] <= SMALL
            return small[:, at[0] - n:at[0]]

        half_c = sm(64)
        ms, rs = sm(64), sm(64)
        ssx = sm(2)
        mx, negm, psum_, rsum, esink = sm(8), sm(8), sm(8), sm(8), sm(8)
        lamv, lame, nlam = sm(2), sm(2), sm(1)
        sinkb = sm(8)
        bst, bmv = sm(24), sm(4)
        rotc, rots = sm(TB * ROT), sm(TB * ROT)
        lg, m8, ixf = sm(16), sm(16), sm(16)
        dv, ev, w0, w1 = sm(2), sm(2), sm(2), sm(2)
        CW, MSK, POS = sm(16), sm(16), sm(16)
        oh0, oh1, tmp8 = sm(16), sm(16), sm(16)
        cntm = sm(8)
        kr1, kr2 = sm(TB * MROPE), sm(TB * MROPE)
        iota8 = sm(8)
        iota = sb("iota", [P, S])
        tri = sb("tri", [P, P])
        ones = sb("ones", [P, P])
        namask = sb("namask", [P, GRID_W])

        raw_in = [sem(f"raw_in{i}") for i in range(RAW)]
        hi_done = sem("hi_done")
        lo_done = sem("lo_done")
        w_used = sem("w_used")
        c_in = sem("c_in")
        x_in = sem("x_in")
        tab_in = sem("tab_in")
        lnb_in = sem("lnb_in")
        bg_in = sem("bg_in")
        bt_in = [sem(f"bt_in{i}") for i in range(NBT)]
        bt_ready = sem("bt_ready")
        out_done = sem("out_done")
        half_set = sem("half_set")
        dve_step = sem("dve_step")
        ms_ready = sem("ms_ready")
        rs_ready = sem("rs_ready")
        tp_src = sem("tp_src")
        tp_full = sem("tp_full")
        tp_hi = sem("tp_hi")
        tp_lo = sem("tp_lo")
        acc_act = sem("acc_act")
        acc_dve = sem("acc_dve")
        qk_src = sem("qk_src")
        qk_full = sem("qk_full")
        qk_act = sem("qk_act")
        qk_dve = sem("qk_dve")
        s_full = sem("s_full")
        mx_done = sem("mx_done")
        p_ready = sem("p_ready")
        pt_full = sem("pt_full")
        pt_act = sem("pt_act")
        pt_dve = sem("pt_dve")
        o_full = sem("o_full")
        o_done = sem("o_done")
        lam_sum, lam_exp = sem("lam_sum"), sem("lam_exp")
        sil_done = sem("sil_done")
        h_ready = sem("h_ready")
        ht_full = sem("ht_full")
        ht_hi = sem("ht_hi")
        ht_lo = sem("ht_lo")
        rw_split = sem("rw_split")
        lg_full = sem("lg_full")
        top_done = sem("top_done")
        exp_done = sem("exp_done")
        route = sem("route")
        pos_full = sem("pos_full")
        plan_done = sem("plan_done")
        se_ready = sem("se_ready")
        xe_full = sem("xe_full")
        xe_hi = sem("xe_hi")
        xe_lo = sem("xe_lo")
        swt_ready = sem("swt_ready")
        ye_ready = sem("ye_ready")
        sc_full = sem("sc_full")
        sc_done = sem("sc_done")
        x_final = sem("x_final")

        def split_hi(e, st, d, limit):
            s, n = st.half(d)
            if s >= limit:
                return
            slot = s // 2 % RAW
            if s % 2 == 0:
                e.wait_ge(raw_in[slot], (n + (s // PERIOD + 1)) * 16)
            wait(e, w_used, st.done(d) - SPLIT)
            nc.scalar.copy(w_hi[:, s % SPLIT, :], raw[:, slot, s % 2 * HALF:(s % 2 + 1) * HALF]).then_inc(hi_done, 1)

        def split_lo(e, st, d, limit):
            s, n = st.half(d)
            if s >= limit:
                return
            slot = s // 2 % RAW
            e.wait_ge(hi_done, st.done(d))
            e.tensor_tensor(w_lo[:, s % SPLIT, :], raw[:, slot, s % 2 * HALF:(s % 2 + 1) * HALF],
                            w_hi[:, s % SPLIT, :].bitcast(F32), ALU.subtract).then_inc(lo_done, 1)

        class Eng:

            def __init__(self, e, kind):
                self.e, self.kind = e, kind
                self.st = Stream()
                self.limit = H_DENSE
                self.src, self.tp = Count(), Count()
                self.acc = Count()
                self.rs = Count()
                self.qks, self.qk = Count(), Count()
                self.map = Count()
                self.ff = Count()
                self.ln = Count()
                self.chain = Count()

            def link(self, ins):
                ins.then_inc(dve_step, 1)
                self.chain.n += 1
                self.e.wait_ge(dve_step, self.chain.at())

            def half_step(self, use=None):
                if self.kind == "pe":
                    s, _ = self.st.half()
                    self.e.wait_ge(lo_done, self.st.done())
                    use(w_hi[:, s % SPLIT, :], w_lo[:, s % SPLIT, :]).then_inc(w_used, 1)
                elif self.kind == "act":
                    split_hi(self.e, self.st, AHEAD, self.limit)
                elif self.kind == "dve":
                    split_lo(self.e, self.st, AHEAD, self.limit)
                self.st.s += 1

            def prologue(self):
                for d in range(AHEAD):
                    if self.kind == "act":
                        split_hi(self.e, self.st, d, self.limit)
                    elif self.kind == "dve":
                        split_lo(self.e, self.st, d, self.limit)

        def mm3(pe, out, xh, xl, wh, wl, first, last):
            pe.matmul(out, xh, wh, start=first, stop=False)
            pe.matmul(out, xh, wl, start=False, stop=False)
            return pe.matmul(out, xl, wh, start=False, stop=last)

        def tp_stage(E, src, blocks, k0, gain=None):
            e = E.e
            if E.kind == "pe":
                wait(e, tp_src, E.src.at(1))
            E.src.n += 1
            for b0 in range(0, blocks, 2):
                nb = min(2, blocks - b0)
                pb = bank[4 + E.tp.n % 4][:, 0:nb * S]
                if E.kind == "pe":
                    wait(e, tp_lo, E.tp.at(1 - 4))
                    for b in range(nb):
                        for tb in range(TB):
                            i = e.transpose(pb[:, b * S + tb * P:b * S + (tb + 1) * P],
                                            src[:, tb, (b0 + b) * P:(b0 + b + 1) * P], ident[:, :])
                    i.then_inc(tp_full, 1)
                elif E.kind == "act":
                    e.wait_ge(tp_full, E.tp.at(1))
                    if gain is None:
                        i = nc.scalar.copy(x_hi[:, k0 + b0:k0 + b0 + nb, :], pb.rearrange("p (b n) -> p b n", n=S))
                    else:
                        for b in range(nb):
                            i = nc.scalar.activation(x_hi[:, k0 + b0 + b, :], pb[:, b * S:(b + 1) * S], ACT.Copy,
                                                     scale=gain[:, b0 + b:b0 + b + 1])
                    i.then_inc(tp_hi, 1)
                elif E.kind == "dve":
                    e.wait_ge(tp_hi, E.tp.at(1))
                    if gain is None:
                        i = e.tensor_tensor(x_lo[:, k0 + b0:k0 + b0 + nb, :], pb.rearrange("p (b n) -> p b n", n=S),
                                            x_hi[:, k0 + b0:k0 + b0 + nb, :].bitcast(F32), ALU.subtract)
                    else:
                        for b in range(nb):
                            i = e.scalar_tensor_tensor(x_lo[:, k0 + b0 + b, :], pb[:, b * S:(b + 1) * S],
                                                       gain[:, b0 + b:b0 + b + 1],
                                                       x_hi[:, k0 + b0 + b, :].bitcast(F32), ALU.mult, ALU.subtract)
                    i.then_inc(tp_lo, 1)
                E.tp.n += 1
            if E.kind == "pe":
                e.wait_ge(tp_lo, E.tp.at())

        def rsqrt(E, n):
            if E.kind == "pool":
                E.e.wait_ge(ms_ready, E.rs.at(1))
                E.e.tensor_tensor(rs[:, 0:n], ms[:, 0:n], half_c[:, 0:n], ALU.pow).then_inc(rs_ready, 1)
            elif E.kind == "dve":
                E.e.wait_ge(rs_ready, E.rs.at(1))
            E.rs.n += 1

        def rms_x(E):
            e = E.e
            if E.kind == "dve":
                for tb in range(TB):
                    i = e.tensor_tensor_reduce(XS[:, tb, :], X[:, tb, :], X[:, tb, :], 1.0, 0.0, ALU.mult, ALU.add,
                                               ssx[:, tb:tb + 1])
                E.link(i)
                e.tensor_scalar(ms[:, 0:2], ssx[:, 0:2], 1.0 / D, EPS, ALU.mult, ALU.add).then_inc(ms_ready, 1)
            rsqrt(E, 2)
            if E.kind == "dve":
                for tb in range(TB):
                    i = e.tensor_scalar(XS[:, tb, :], X[:, tb, :], rs[:, tb:tb + 1], None, ALU.mult)
                i.then_inc(tp_src, 1)

        def gemm_cols(E, width, evac_act, evac_dve, kn=KD):
            e = E.e
            b = 2 * (E.acc.n % 2)
            per = HALF // width if kn == KD else 1
            nh = kn // per
            if width == 288 or width == 384:
                nh, per = kn // 2, 2
            if E.kind == "pe":
                wait(e, acc_act, E.acc.at(1 - 2))
                wait(e, acc_dve, E.acc.at(1 - 2))
            for hx in range(nh):
                def use(wh, wl, hx=hx):
                    stride = HALF // per
                    for j in range(per):
                        k = hx * per + j
                        w = slice(j * stride, j * stride + width)
                        for tb in range(TB):
                            t = slice(tb * P, (tb + 1) * P)
                            i = mm3(e, bank[b + tb][:, 0:width], x_hi[:, k, t], x_lo[:, k, t], wh[:, w], wl[:, w],
                                    k == 0, k == kn - 1)
                    return i
                E.half_step(use)
            if E.kind == "act":
                e.wait_ge(w_used, E.st.done(-1))
                evac_act(bank[b]).then_inc(acc_act, 1)
            if E.kind == "dve":
                e.wait_ge(w_used, E.st.done(-1))
                evac_dve(bank[b + 1]).then_inc(acc_dve, 1)
            E.acc.n += 1

        def gemm_rows(E, nh, k0, b0=4, last_wait=None):
            e = E.e
            for hx in range(nh):
                def use(wh, wl, hx=hx):
                    for tb in range(TB):
                        t = slice(tb * P, (tb + 1) * P)
                        for c in range(2):
                            w = slice(c * 512, (c + 1) * 512)
                            i = mm3(e, bank[b0 + 2 * tb + c][:, :], x_hi[:, k0 + hx, t], x_lo[:, k0 + hx, t],
                                    wh[:, w], wl[:, w], hx == 0, hx == nh - 1)
                    return i
                E.half_step(use)

        def scalar_rows(E, fn, b0=4):
            if E.kind == "dve":
                E.e.wait_ge(w_used, E.st.done(-1))
                for tb in range(TB):
                    for c in range(2):
                        fn(tb, c, bank[b0 + 2 * tb + c][:, :])

        def rope(E, x, heads, dim, ct, stb, parts, r, dst=None):
            e = E.e
            dst = x if dst is None else dst
            c = ct.unsqueeze(1).to_broadcast([P, heads, dim])
            y = t1[:, 0:heads * dim].rearrange("p (h d) -> p h d", h=heads)
            z = t2[:, 0:heads * dim].rearrange("p (h d) -> p h d", h=heads)
            e.tensor_tensor(y, x, c, ALU.mult)
            for a, w in parts:
                h = w // 2
                for i0, i1 in ((a, a + h), (a + h, a)):
                    i = e.tensor_tensor(z[:, :, i0:i0 + h], x[:, :, i1:i1 + h],
                                        stb[:, i0:i0 + h].unsqueeze(1).to_broadcast([P, heads, h]), ALU.mult)
            E.link(i)
            lo, hi = parts[0][0], parts[-1][0] + parts[-1][1]
            E.link(e.tensor_tensor(y[:, :, lo:hi], y[:, :, lo:hi], z[:, :, lo:hi], ALU.add))
            if r is None:
                return e.tensor_copy(dst, y)
            return e.tensor_tensor(dst, y, r.unsqueeze(2).to_broadcast([P, heads, dim]), ALU.mult)

        def qk_stage(E, units, dst, scaled=()):
            e = E.e
            if E.kind == "pe":
                wait(e, qk_src, E.qks.at(1))
            E.qks.n += 1
            for u, blocks in enumerate(units):
                pb = bank[4 + E.qk.n % 4]
                mine = E.qk.n % 2
                if E.kind == "pe":
                    wait(e, (qk_act, qk_dve)[mine], (E.qk.n - 4) // 2 + 1)
                    for b, (blk, src, w) in enumerate(blocks):
                        for tb in range(TB):
                            i = e.transpose(pb[0:w, b * S + tb * P:b * S + (tb + 1) * P], src(tb), ident[:, :])
                    i.then_inc(qk_full, 1)
                elif E.kind == ("act", "dve")[mine]:
                    e.wait_ge(qk_full, E.qk.at(1))
                    for b, (blk, src, w) in enumerate(blocks):
                        o, p = dst[0:w, blk, :], pb[0:w, b * S:(b + 1) * S]
                        if blk in scaled:
                            i = nc.scalar.mul(o, p, HD ** -0.5) if mine == 0 else e.tensor_scalar(
                                o, p, HD ** -0.5, None, ALU.mult)
                        else:
                            i = nc.scalar.copy(o, p) if mine == 0 else e.tensor_copy(o, p)
                    i.then_inc((qk_act, qk_dve)[mine], 1)
                E.qk.n += 1

        def attention(E, maps):
            e = E.e
            M = len(maps)
            if E.kind == "pe":
                wait(e, qk_act, (E.qk.n + 1) // 2)
                wait(e, qk_dve, E.qk.n // 2)
                wait(e, acc_act, E.acc.at())
                wait(e, acc_dve, E.acc.at())
            for step in range(M + 2):
                m = step
                if m < M:
                    a = maps[m]
                    sbk = bank[m % 2]
                    g = E.map.at(m)
                    sc2 = slice(2 * (m % 4), 2 * (m % 4) + 2)
                    if E.kind == "pe":
                        wait(e, p_ready, g + 1 - 2)
                        (qb, q0, q1), (kb, k0, k1), Q = a["q"], a["k"], a["qk"]
                        for tb in range(TB):
                            i = e.matmul(sbk[:, tb * S:(tb + 1) * S], Q[q0:q1, qb, tb * P:(tb + 1) * P],
                                         Q[k0:k1, kb, :], start=True, stop=True)
                        i.then_inc(s_full, 1)
                    if E.kind == "dve":
                        e.wait_ge(s_full, g + 1)
                        if "bias" in a:
                            a["bias_wait"](E)
                            wait(e, p_ready, g + 1 - 2)
                            for tb in range(TB):
                                i = e.tensor_tensor_reduce(SS[:, m % 2, tb, :], sbk[:, tb * S:(tb + 1) * S],
                                                           a["bias"][:, tb, :], 1.0, -3.0e38, ALU.add, ALU.max,
                                                           mx[:, 2 * (m % 4) + tb:2 * (m % 4) + tb + 1])
                            E.link(i)
                            if "sink" in a:
                                E.link(e.tensor_scalar(mx[:, sc2], mx[:, sc2], a["sink"], None, ALU.max))
                        else:
                            E.link(e.tensor_reduce(mx[:, sc2], sbk[:, :].rearrange("p (t n) -> p t n", t=TB),
                                                   AX.X, ALU.max))
                        e.tensor_scalar(negm[:, sc2], mx[:, sc2], -a["scale"], None, ALU.mult).then_inc(mx_done, 1)
                    if E.kind == "act":
                        e.wait_ge(mx_done, g + 1)
                        wait(e, pt_full, g + 1 - 2)
                        if "sink" in a:
                            nc.scalar.activation(esink[:, sc2], negm[:, sc2], ACT.Exp, bias=a["sink"], scale=1.0)
                        for tb in range(TB):
                            src = SS[:, m % 2, tb, :] if "bias" in a else sbk[:, tb * S:(tb + 1) * S]
                            j = 2 * (m % 4) + tb
                            i = nc.scalar.activation(PP[:, m % 2, tb, :], src, ACT.Exp, bias=negm[:, j:j + 1],
                                                     scale=a["scale"], accum_out=psum_[:, j:j + 1])
                        i.then_inc(p_ready, 1)
                m = step - 1
                if 0 <= m < M:
                    g = E.map.at(m)
                    tbk = bank[2 + m % 2]
                    if E.kind == "pe":
                        e.wait_ge(p_ready, g + 1)
                        wait(e, (pt_act, pt_dve)[m % 2], g // 2)
                        for kb in range(TB):
                            for tb in range(TB):
                                i = e.transpose(tbk[:, kb * S + tb * P:kb * S + (tb + 1) * P],
                                                PP[:, m % 2, tb, kb * P:(kb + 1) * P], ident[:, :])
                        i.then_inc(pt_full, 1)
                    if E.kind == ("act", "dve")[m % 2]:
                        e.wait_ge(pt_full, g + 1)
                        wait(e, o_full, g + 1 - 2)
                        src = tbk[:, :].rearrange("p (k n) -> p k n", k=TB)
                        if E.kind == "act":
                            nc.scalar.copy(PT[:, m % 2, :, :], src).then_inc(pt_act, 1)
                        else:
                            e.tensor_copy(PT[:, m % 2, :, :], src).then_inc(pt_dve, 1)
                m = step - 2
                if 0 <= m < M:
                    a = maps[m]
                    g = E.map.at(m)
                    w = a["width"]
                    ob = bank[4 + m % 4]
                    sc2 = slice(2 * (m % 4), 2 * (m % 4) + 2)
                    if E.kind == "pe":
                        e.wait_ge((pt_act, pt_dve)[m % 2], g // 2 + 1)
                        wait(e, o_done, g + 1 - 4)
                        for tb in range(TB):
                            for kb in range(TB):
                                i = e.matmul(ob[:, tb * w:(tb + 1) * w], PT[:, m % 2, kb, tb * P:(tb + 1) * P],
                                             a["v"](kb), start=kb == 0, stop=kb == TB - 1)
                        i.then_inc(o_full, 1)
                    if E.kind == "dve":
                        if "sink" in a:
                            E.link(e.tensor_tensor(psum_[:, sc2], psum_[:, sc2], esink[:, sc2], ALU.add))
                        E.link(e.reciprocal(rsum[:, sc2], psum_[:, sc2]))
                        if a.get("minus"):
                            E.link(e.tensor_scalar(rsum[:, sc2], rsum[:, sc2], nlam[:, 0:1], None, ALU.mult))
                        e.wait_ge(o_full, g + 1)
                        src = ob[:, 0:TB * w].rearrange("p (t n) -> p t n", t=TB)
                        r = rsum[:, sc2].unsqueeze(2).to_broadcast([P, TB, w])
                        if a.get("minus"):
                            tt = t3[:, 0:TB * w].rearrange("p (t n) -> p t n", t=TB)
                            E.link(e.tensor_tensor(tt, src, r, ALU.mult))
                            i = e.tensor_tensor(a["out"], a["out"], tt, ALU.add)
                        else:
                            i = e.tensor_tensor(a["out"], src, r, ALU.mult)
                        i.then_inc(o_done, 1)
            E.map.n += M

        def drain_dve(E):
            if E.kind == "dve":
                E.link(E.e.engine_nop())

        def copy_act(dst):
            return lambda b: nc.scalar.copy(dst, b)

        def first_layer(E, l):
            e = E.e
            if E.kind == "dve":
                e.wait_ge(tab_in, (l + 1) * 48)
                for ta, g in ((CT, rowv[:, R_G:R_G + ROPEW]), (ST, rowv[:, R_GS:R_GS + ROPEW])):
                    e.tensor_tensor(ta, ta, g.unsqueeze(1).to_broadcast([P, TB, ROPEW]), ALU.mult)
                for j in range(2):
                    a = R_LAM + 2 * j * DQ
                    i = e.tensor_tensor_reduce(t1[:, 0:DQ], rowv[:, a:a + DQ], rowv[:, a + DQ:a + 2 * DQ], 1.0, 0.0,
                                               ALU.mult, ALU.add, lamv[:, j:j + 1])
                    E.link(i)
                e.engine_nop().then_inc(lam_sum, 1)
            if E.kind == "act":
                e.wait_ge(lam_sum, l + 1)
                nc.scalar.activation(lame[:, :], lamv[:, :], ACT.Exp).then_inc(lam_exp, 1)
            lambda_init = 0.8 - 0.6 * math.exp(-0.3 * l)
            if E.kind == "dve":
                e.wait_ge(lam_exp, l + 1)
                E.link(e.tensor_tensor(nlam[:, :], lame[:, 1:2], lame[:, 0:1], ALU.subtract))
                E.link(e.tensor_scalar(nlam[:, :], nlam[:, :], -lambda_init, None, ALU.add))
            rms_x(E)
            tp_stage(E, XS, KD, 0, colg[:, l, CG_ATTN:CG_ATTN + KD])
            for c, w in chunks_in1():
                gemm_cols(E, w, lambda b, c=c, w=w: nc.scalar.copy(H[:, 0, c:c + w], b[:, 0:w]),
                          lambda b, c=c, w=w: e.tensor_copy(H[:, 1, c:c + w], b[:, 0:w]))
            if E.kind == "dve":
                e.wait_ge(acc_act, E.acc.at())
                drain_dve(E)
                for j, (c, w) in enumerate(((C_CQ, MQR), (C_CKV, MKVR))):
                    for tb in range(TB):
                        i = e.tensor_tensor_reduce(t1[:, 0:w], H[:, tb, c:c + w], H[:, tb, c:c + w], 1.0 / w, EPS,
                                                   ALU.mult, ALU.add, ms[:, 2 * j + tb:2 * j + tb + 1])
                        E.link(i)
                e.engine_nop().then_inc(ms_ready, 1)
            rsqrt(E, 4)
            if E.kind == "dve":
                for j, (c, w) in enumerate(((C_CQ, MQR), (C_CKV, MKVR))):
                    for tb in range(TB):
                        i = e.tensor_scalar(XS[:, tb, c:c + w], H[:, tb, c:c + w], rs[:, 2 * j + tb:2 * j + tb + 1],
                                            None, ALU.mult)
                i.then_inc(tp_src, 1)
            nq, nk = MQR // P, MKVR // P
            tp_stage(E, XS[:, :, 0:MQR + MKVR], nq + nk, 0, colg[:, l, CG_Q:CG_Q + nq + nk])
            for kn, kk, w, dst in ((nq, 0, MH * MQK // 2, QA), (nk, nq, MH * (MNOPE + MV) // 2, KV)):
                b = 0
                if E.kind == "pe":
                    wait(e, acc_act, E.acc.at())
                    wait(e, acc_dve, E.acc.at())
                for hx in range(kn):
                    def use(wh, wl, hx=hx, w=w, kn=kn, kk=kk):
                        for c in range(2):
                            for tb in range(TB):
                                t = slice(tb * P, (tb + 1) * P)
                                i = mm3(e, bank[2 * c + tb][:, 0:w], x_hi[:, kk + hx, t], x_lo[:, kk + hx, t],
                                        wh[:, c * w:(c + 1) * w], wl[:, c * w:(c + 1) * w], hx == 0, hx == kn - 1)
                        return i
                    E.half_step(use)
                E.acc.n += 1
                for c in range(2):
                    if E.kind == "act":
                        if c == 0:
                            e.wait_ge(w_used, E.st.done(-1))
                        i = nc.scalar.copy(dst[:, 0, c * w:(c + 1) * w], bank[2 * c][:, 0:w])
                    if E.kind == "dve":
                        if c == 0:
                            e.wait_ge(w_used, E.st.done(-1))
                        i = e.tensor_copy(dst[:, 1, c * w:(c + 1) * w], bank[2 * c + 1][:, 0:w])
                if E.kind == "act":
                    i.then_inc(acc_act, 1)
                if E.kind == "dve":
                    i.then_inc(acc_dve, 1)
            nd, ng = 4 * DH, GH + GKV
            if E.kind == "dve":
                e.wait_ge(acc_act, E.acc.at())
                drain_dve(E)
                per = nd + ng + 2 * MH
                for tb in range(TB):
                    o = tb * 32
                    jobs = [(H[:, tb, C_DQ:C_DV], nd, DQ, o), (H[:, tb, C_GQ:C_GV], ng, GD, o + nd)]
                    for j, (x, n, d, a) in enumerate(jobs):
                        for s0 in range(0, n, 8):
                            y = t1[:, 0:8 * d]
                            E.link(e.tensor_tensor(y, x[:, s0 * d:(s0 + 8) * d], x[:, s0 * d:(s0 + 8) * d], ALU.mult))
                            E.link(e.tensor_reduce(ms[:, a + s0:a + s0 + 8], y.rearrange("p (h d) -> p h d", d=d),
                                                   AX.X, ALU.add))
                i = e.tensor_scalar(ms[:, :], ms[:, :], 1.0 / DQ, EPS, ALU.mult, ALU.add)
                i.then_inc(ms_ready, 1)
            rsqrt(E, 64)
            if E.kind == "dve":
                for tb in range(TB):
                    o = tb * 32
                    for k, (c, n, f, parts) in enumerate((
                            (C_DQ, 2 * DH, F_DQ, [(0, DQ)]), (C_DK, 2 * DH, F_DK, [(0, DQ)]),
                            (C_GQ, GH, F_GQ, [(0, GD // 2), (GD // 2, GD // 2)]),
                            (C_GK, GKV, F_GK, [(0, GD // 2), (GD // 2, GD // 2)]))):
                        x = H[:, tb, c:c + n * 64].rearrange("p (h d) -> p h d", h=n)
                        E.link(rope(E, x, n, 64, CT[:, tb, f:f + 64], ST[:, tb, f:f + 64], parts, rs[:, o:o + n]))
                        o += n
                for tb in range(TB):
                    o = tb * 16
                    y = t1[:, 0:MH * MQK]
                    E.link(e.tensor_tensor(y, QA[:, tb, :], QA[:, tb, :], ALU.mult))
                    E.link(e.tensor_reduce(ms[:, o:o + MH], y.rearrange("p (h d) -> p h d", d=MQK), AX.X, ALU.add))
                    kn = KV[:, tb, :].rearrange("p (h d) -> p h d", h=MH)[:, :, 0:MNOPE]
                    y = t1[:, 0:MH * MNOPE].rearrange("p (h d) -> p h d", h=MH)
                    E.link(e.tensor_tensor(y, kn, kn, ALU.mult))
                    kr = H[:, tb, C_KR:C_KR + MROPE]
                    E.link(e.tensor_tensor_reduce(t2[:, 0:MROPE], kr, kr, 1.0, 0.0, ALU.mult, ALU.add,
                                                  ssx[:, tb:tb + 1]))
                    E.link(e.tensor_reduce(ms[:, o + MH:o + 2 * MH], y, AX.X, ALU.add))
                    E.link(e.tensor_scalar(ms[:, o + MH:o + 2 * MH], ms[:, o + MH:o + 2 * MH], ssx[:, tb:tb + 1],
                                           None, ALU.add))
                e.tensor_scalar(ms[:, 0:32], ms[:, 0:32], 1.0 / MQK, EPS, ALU.mult, ALU.add).then_inc(ms_ready, 1)
            rsqrt(E, 32)
            if E.kind == "dve":
                for tb in range(TB):
                    o = tb * 16
                    x = QA[:, tb, :].rearrange("p (h d) -> p h d", h=MH)
                    E.link(rope(E, x, MH, MQK, CT[:, tb, F_MQ:F_MQ + MQK], ST[:, tb, F_MQ:F_MQ + MQK],
                                [(MNOPE, MROPE)], rs[:, o:o + MH]))
                    kr = H[:, tb, C_KR:C_KR + MROPE].unsqueeze(1)
                    a = F_MK + MNOPE
                    krr = kr1[:, tb * MROPE:(tb + 1) * MROPE].unsqueeze(1)
                    E.link(rope(E, kr, 1, MROPE, CT[:, tb, a:a + MROPE], ST[:, tb, a:a + MROPE], [(0, MROPE)], None,
                                dst=krr))
                    ka = KA[:, tb, :].rearrange("p (h d) -> p h d", h=MH)
                    kn = KV[:, tb, :].rearrange("p (h d) -> p h d", h=MH)[:, :, 0:MNOPE]
                    y = t1[:, 0:MH * MNOPE].rearrange("p (h d) -> p h d", h=MH)
                    E.link(e.tensor_tensor(y, kn, CT[:, tb, F_MK:F_MK + MNOPE].unsqueeze(1).to_broadcast(
                        [P, MH, MNOPE]), ALU.mult))
                    r = rs[:, o + MH:o + 2 * MH].unsqueeze(2)
                    e.tensor_tensor(ka[:, :, 0:MNOPE], y, r.to_broadcast([P, MH, MNOPE]), ALU.mult)
                    E.link(e.tensor_tensor(ka[:, :, MNOPE:MQK], krr.to_broadcast([P, MH, MROPE]),
                                           r.to_broadcast([P, MH, MROPE]), ALU.mult))
                e.engine_nop().then_inc(qk_src, 1)
            def blk(src, c, w):
                return lambda tb: src[:, tb, c:c + w]
            blocks = [(j, blk(H, C_DQ + j * P, P), P) for j in range(2 * DH)]
            nb = 2 * DH
            gg = GH // GKV
            blocks += [(nb + j, blk(H, C_GQ + j * P, P), P) for j in range(gg + 1)]
            nb += (GH + GKV) // 2
            blocks += [(nb + j, blk(QA, j * MQK, MQK), MQK) for j in range(MH)]
            blocks += [(nb + MH + j, blk(KA, j * MQK, MQK), MQK) for j in range(MH)]
            qk_stage(E, [blocks[j:j + 2] for j in range(0, len(blocks), 2)], QK1)
            maps = []
            for h in range(DH):
                for c in range(2):
                    o = MH * MV + h * DV
                    maps.append(dict(q=(h, c * 64, c * 64 + 64), k=(DH + h, c * 64, c * 64 + 64), qk=QK1,
                                     scale=DQ ** -0.5, width=DV, minus=c == 1,
                                     v=lambda kb, h=h: H[:, kb, C_DV + h * DV:C_DV + (h + 1) * DV],
                                     out=O[:, :, o:o + DV]))
            for h in range(GH):
                kv = h // gg
                maps.append(dict(q=(2 * DH + h % gg, kv * 64, kv * 64 + 64), k=(2 * DH + gg, kv * 64, kv * 64 + 64),
                                 qk=QK1, scale=GD ** -0.5, width=GD,
                                 v=lambda kb, kv=kv: H[:, kb, C_GV + kv * GD:C_GV + (kv + 1) * GD],
                                 out=O[:, :, MH * MV + DH * DV + h * GD:MH * MV + DH * DV + (h + 1) * GD]))
            for h in range(MH):
                maps.append(dict(q=(nb + h, 0, MQK), k=(nb + MH + h, 0, MQK), qk=QK1, scale=MQK ** -0.5, width=MV,
                                 v=lambda kb, h=h: KV[:, kb, h * P + MNOPE:(h + 1) * P],
                                 out=O[:, :, h * MV:(h + 1) * MV]))
            attention(E, maps)
            if E.kind == "dve":
                drain_dve(E)
                for tb in range(TB):
                    x = O[:, tb, MH * MV:MH * MV + DH * DV]
                    y = t1[:, 0:DH * DV]
                    E.link(e.tensor_tensor(y, x, x, ALU.mult))
                    E.link(e.tensor_reduce(ms[:, tb * DH:(tb + 1) * DH], y.rearrange("p (h d) -> p h d", h=DH),
                                           AX.X, ALU.add))
                e.tensor_scalar(ms[:, 0:2 * DH], ms[:, 0:2 * DH], 1.0 / DV, EPS, ALU.mult, ALU.add).then_inc(
                    ms_ready, 1)
            rsqrt(E, 2 * DH)
            if E.kind == "dve":
                for tb in range(TB):
                    x = O[:, tb, MH * MV:MH * MV + DH * DV].rearrange("p (h d) -> p h d", h=DH)
                    E.link(e.tensor_tensor(x, x, rs[:, tb * DH:(tb + 1) * DH].unsqueeze(2).to_broadcast(
                        [P, DH, DV]), ALU.mult))
                    i = e.scalar_tensor_tensor(x, x, 1.0 - lambda_init, rowv[:, R_OG:R_OG + DV].unsqueeze(
                        1).to_broadcast([P, DH, DV]), ALU.mult, ALU.mult)
                i.then_inc(tp_src, 1)
            tp_stage(E, O, MIX // P, 0)
            gemm_rows(E, MIX // P, 0)
            scalar_rows(E, lambda tb, c, b: e.tensor_tensor(
                X[:, tb, c * 512:(c + 1) * 512], X[:, tb, c * 512:(c + 1) * 512], b, ALU.add))
            drain_dve(E)
            rms_x(E)
            tp_stage(E, XS, KD, 0, colg[:, l, CG_FFN:CG_FFN + KD])
            ffn(E, FF1 // FC, TB)
            scalar_rows(E, lambda tb, c, b: e.tensor_tensor(
                X[:, tb, c * 512:(c + 1) * 512], X[:, tb, c * 512:(c + 1) * 512], b, ALU.add))
            drain_dve(E)

        def ffn(E, nc_, tbs):
            e = E.e
            T = tbs * P
            if E.kind == "pool":
                return

            def gu_half(hx):
                def use(wh, wl):
                    for j in range(2):
                        k = 2 * hx + j
                        w = slice(j * 512, (j + 1) * 512)
                        for tb in range(tbs):
                            t = slice(tb * P, (tb + 1) * P)
                            i = mm3(e, bank[tb][:, :], x_hi[:, k, t], x_lo[:, k, t], wh[:, w], wl[:, w],
                                    k == 0, k == KD - 1)
                    return i
                if E.kind == "pe" and hx == 0:
                    wait(e, h_ready, E.ff.at())
                E.half_step(use)

            def turn(back):
                n = E.ff.at(1 - back)
                tr = [bank[2 + f][:, 0:T] for f in range(2)]
                if E.kind == "pe":
                    e.wait_ge(h_ready, n)
                    for f in range(2):
                        for tb in range(tbs):
                            i = e.transpose(tr[f][:, tb * P:(tb + 1) * P], HH[:, tb, f * P:(f + 1) * P], ident[:, :])
                    i.then_inc(ht_full, 1)
                if E.kind == "act":
                    e.wait_ge(ht_full, n)
                    for f in range(2):
                        i = nc.scalar.copy(hT_hi[:, f, 0:T], tr[f])
                    i.then_inc(ht_hi, 1)
                if E.kind == "dve":
                    e.wait_ge(ht_hi, n)
                    for f in range(2):
                        i = e.tensor_tensor(hT_lo[:, f, 0:T], tr[f], hT_hi[:, f, 0:T].bitcast(F32), ALU.subtract)
                    i.then_inc(ht_lo, 1)

            def act_mul():
                n = E.ff.at(1)
                if E.kind == "act":
                    e.wait_ge(w_used, E.st.done(-1))
                    for tb in range(tbs):
                        i = nc.scalar.activation(SIL[:, tb, :], bank[tb][:, 0:FC], ACT.Silu)
                    i.then_inc(sil_done, 1)
                if E.kind == "dve":
                    e.wait_ge(sil_done, n)
                    for tb in range(tbs):
                        i = e.tensor_tensor(HH[:, tb, :], SIL[:, tb, :], bank[tb][:, FC:2 * FC], ALU.mult)
                    i.then_inc(h_ready, 1)

            def down(hx, first, last):
                def use(wh, wl):
                    for tb in range(tbs):
                        t = slice(tb * P, (tb + 1) * P)
                        for c in range(2):
                            w = slice(c * 512, (c + 1) * 512)
                            i = mm3(e, bank[4 + 2 * tb + c][:, :], hT_hi[:, hx, t], hT_lo[:, hx, t],
                                    wh[:, w], wl[:, w], first and hx == 0, last and hx == 1)
                    return i
                if E.kind == "pe" and hx == 0:
                    e.wait_ge(ht_lo, E.ff.at())
                E.half_step(use)

            def chunk(first=False):
                gu_half(0)
                gu_half(1)
                turn(1)
                gu_half(2)
                gu_half(3)
                act_mul()
                down(0, first, False)
                down(1, first, False)
                E.ff.n += 1

            for hx in range(4):
                gu_half(hx)
            act_mul()
            E.ff.n += 1
            pairs = (nc_ - 1) // 2
            chunk(first=True)
            chunk()
            loops = pairs - 1
            s0, p0 = E.st.s, E.st.periods
            with e.Fori(0, loops) as i:
                E.st.periods = p0 + i
                E.ff.enter(i, 2)
                chunk()
                chunk()
                E.ff.leave(loops)
            E.st.s, E.st.periods = s0 + loops * PERIOD, p0
            if (nc_ - 1) % 2:
                chunk()
            turn(1)
            down(0, False, True)
            down(1, False, True)

        def layer_norm(E):
            e = E.e
            if E.kind == "dve":
                for tb in range(TB):
                    for c in range(2):
                        i = e.bn_stats(bst[:, tb * 12 + c * 6:tb * 12 + c * 6 + 6], X[:, tb, c * 512:(c + 1) * 512])
                E.link(i)
                for tb in range(TB):
                    i = e.bn_aggr(bmv[:, 2 * tb:2 * tb + 2], bst[:, tb * 12:(tb + 1) * 12])
                E.link(i)
                e.tensor_scalar(ms[:, 0:4], bmv[:, 0:4], LN_EPS, 0.0, ALU.add, ALU.max).then_inc(ms_ready, 1)
            rsqrt_var(E)
            if E.kind == "dve":
                e.wait_ge(lnb_in, E.ln.at(1) * 16)
                for tb in range(TB):
                    i = e.tensor_scalar(X[:, tb, :], X[:, tb, :], bmv[:, 2 * tb:2 * tb + 1], rs[:, 2 * tb + 1:2 * tb + 2],
                                        ALU.subtract, ALU.mult)
                E.link(i)
                g = GB[:, 0:D].unsqueeze(1).to_broadcast([P, TB, D])
                b = GB[:, D:2 * D].unsqueeze(1).to_broadcast([P, TB, D])
                E.link(e.tensor_tensor(X[:, :, :], X[:, :, :], g, ALU.mult))
                E.link(e.tensor_tensor(X[:, :, :], X[:, :, :], b, ALU.add))
                e.engine_nop().then_inc(ln_done, 1)
            E.ln.n += 1

        ln_done = sem("ln_done")
        at_done = sem("at_done")

        def rsqrt_var(E):
            if E.kind == "pool":
                E.e.wait_ge(ms_ready, E.rs.at(1))
                for tb in range(TB):
                    i = E.e.tensor_tensor(rs[:, 2 * tb + 1:2 * tb + 2], ms[:, 2 * tb + 1:2 * tb + 2],
                                          half_c[:, 0:1], ALU.pow)
                i.then_inc(rs_ready, 1)
            elif E.kind == "dve":
                E.e.wait_ge(rs_ready, E.rs.at(1))
            E.rs.n += 1

        def second_mixer(E, l):
            e = E.e
            if E.kind == "dve":
                e.engine_nop().then_inc(tp_src, 1)
            tp_stage(E, X, KD, 0)
            n_qkv = len([c for c in chunks_in2() if c[0] < W_QKV2])
            for j, (c, w) in enumerate(chunks_in2()):
                if j < n_qkv:
                    gemm_cols(E, w, lambda b, c=c, w=w: nc.scalar.copy(H2[:, 0, c:c + w], b[:, 0:w]),
                              lambda b, c=c, w=w: e.tensor_copy(H2[:, 1, c:c + w], b[:, 0:w]))
                else:
                    g = c - W_QKV2
                    bias = (BG if g < D else BG2)[:, g % D:g % D + 512]

                    def both(b, g=g, bias=bias):
                        if E.acc.n % 2 == 0:
                            b0, b1 = bank[0], bank[1]
                        else:
                            b0, b1 = bank[2], bank[3]
                        e.wait_ge(bg_in, (l + 1) * 64)
                        e.tensor_tensor(G2[:, 0, g:g + 512], b0[:, :], bias, ALU.add)
                        return e.tensor_tensor(G2[:, 1, g:g + 512], b1[:, :], bias, ALU.add)

                    def gates(b, g=g):
                        e.wait_ge(acc_dve, E.acc.at(1))
                        return nc.scalar.activation(G2[:, :, g:g + 512], G2[:, :, g:g + 512], ACT.Sigmoid)
                    gemm_cols(E, w, gates, both)
            if E.kind == "dve":
                e.wait_ge(acc_act, E.acc.at())
                drain_dve(E)
                n = SH + SKV
                for tb in range(TB):
                    x = H2[:, tb, C_QS:C_VS].rearrange("p (h d) -> p h d", h=n)[:, :, 0:ROT]
                    c = rotc[:, tb * ROT:(tb + 1) * ROT].unsqueeze(1).to_broadcast([P, n, ROT])
                    y = t1[:, 0:n * ROT].rearrange("p (h d) -> p h d", h=n)
                    z = t2[:, 0:n * ROT].rearrange("p (h d) -> p h d", h=n)
                    e.tensor_tensor(y, x, c, ALU.mult)
                    h = ROT // 2
                    for i0, i1 in ((0, h), (h, 0)):
                        i = e.tensor_tensor(z[:, :, i0:i0 + h], x[:, :, i1:i1 + h],
                                            rots[:, tb * ROT + i0:tb * ROT + i0 + h].unsqueeze(1).to_broadcast(
                                                [P, n, h]), ALU.mult)
                    E.link(i)
                    E.link(e.tensor_tensor(x, y, z, ALU.add))
                e.engine_nop().then_inc(qk_src, 1)

            def blk(c):
                return lambda tb: H2[:, tb, c:c + P]
            blocks = [(j, blk(j * P), P) for j in range(NH)]
            sg = SH // SKV
            blocks += [(NH + j, blk(C_QS + j * P), P) for j in range(sg + 1)]
            scaled = set(range(NH // 2)) | {NH + j for j in range(SH // 2)}
            qk_stage(E, [blocks[j:j + 2] for j in range(0, len(blocks), 2)], QK2, scaled)
            maps = []
            for h in range(NH):
                p0 = h % 2 * 64

                def bias_wait(E, h=h):
                    E.e.wait_ge(bt_ready, l * NH + h + 1)
                maps.append(dict(q=(h // 2, p0, p0 + 64), k=(NH // 2 + h // 2, p0, p0 + 64), qk=QK2, scale=1.0,
                                 width=HD, bias=BT[:, h % (NBT - 1)], bias_wait=bias_wait,
                                 v=lambda kb, h=h: H2[:, kb, 2 * W_NA + h * HD:2 * W_NA + (h + 1) * HD],
                                 out=O[:, :, h * HD:(h + 1) * HD]))
            for h in range(SH):
                kv = h // sg
                maps.append(dict(q=(NH + h % sg, kv * 64, kv * 64 + 64), k=(NH + sg, kv * 64, kv * 64 + 64), qk=QK2,
                                 scale=1.0, width=HD, bias=BT[:, NBT - 1], bias_wait=lambda E: None,
                                 sink=sinkb[:, h:h + 1],
                                 v=lambda kb, kv=kv: H2[:, kb, C_VS + kv * HD:C_VS + (kv + 1) * HD],
                                 out=O[:, :, W_NA + h * HD:W_NA + (h + 1) * HD]))
            if E.kind == "dve":
                e.wait_ge(bg_in, (l + 1) * 64)
            attention(E, maps)
            if E.kind == "dve":
                e.engine_nop().then_inc(tp_src, 1)
            tp_stage(E, O[:, :, 0:D], KD, 0)
            gemm_rows(E, W_NA // P, 0)
            scalar_rows(E, lambda tb, c, b: e.tensor_tensor(
                YG[:, tb, c * 512:(c + 1) * 512], b, G2[:, tb, c * 512:(c + 1) * 512], ALU.mult))
            if E.kind == "dve":
                drain_dve(E)
            gemm_rows(E, W_NA // P, W_NA // P, b0=0)

            def add_sw(tb, c, b):
                g = G2[:, tb, D + c * 512:D + (c + 1) * 512]
                E.link(e.tensor_tensor(t1[:, 0:512], b, g, ALU.mult))
                E.link(e.tensor_tensor(YG[:, tb, c * 512:(c + 1) * 512], YG[:, tb, c * 512:(c + 1) * 512],
                                       t1[:, 0:512], ALU.add))

            scalar_rows(E, add_sw, b0=0)
            if E.kind == "dve":
                e.engine_nop().then_inc(tp_src, 1)
            tp_stage(E, YG, KD, 0)
            gemm_rows(E, KD, 0)
            residual(E)
            layer_norm(E)

        def residual(E):
            scalar_rows(E, lambda tb, c, b: E.e.scalar_tensor_tensor(
                X[:, tb, c * 512:(c + 1) * 512], X[:, tb, c * 512:(c + 1) * 512], ALPHA, b, ALU.mult, ALU.add))
            drain_dve(E)

        def moe(E):
            e = E.e
            if E.kind == "pool":
                return
            if E.kind == "dve":
                e.engine_nop().then_inc(tp_src, 1)
            tp_stage(E, X, KD, 0)
            if E.kind == "act":
                e.wait_ge(bt_in[2], 16)
                nc.scalar.copy(rw_hi[:, :, :], T2[:, 0:KD * NE].rearrange("p (k n) -> p k n", n=NE)).then_inc(
                    rw_split, 1)
            if E.kind == "dve":
                e.wait_ge(rw_split, 1)
                e.tensor_tensor(rw_lo[:, :, :], T2[:, 0:KD * NE].rearrange("p (k n) -> p k n", n=NE),
                                rw_hi[:, :, :].bitcast(F32), ALU.subtract).then_inc(rw_split, 1)
            if E.kind == "pe":
                e.wait_ge(rw_split, 2)
                e.wait_ge(tp_lo, E.tp.at())
                for tb in range(TB):
                    t = slice(tb * P, (tb + 1) * P)
                    n = 0
                    for k in range(KD):
                        for a in (x_hi, x_lo):
                            for b in (rw_hi, rw_lo):
                                i = e.matmul(bank[tb][:, 0:NE], a[:, k, t], b[:, k, :], start=n == 0,
                                             stop=n == 4 * KD - 1)
                                n += 1
                i.then_inc(lg_full, 1)
            if E.kind == "dve":
                e.wait_ge(lg_full, 1)
                for tb in range(TB):
                    i = e.tensor_copy(lg[:, tb * 8:(tb + 1) * 8], bank[tb][:, 0:NE])
                E.link(i)
                for tb in range(TB):
                    i = e.max(m8[:, tb * 8:(tb + 1) * 8], lg[:, tb * 8:(tb + 1) * 8])
                E.link(i)
                for tb in range(TB):
                    i = e.max_index(idx[:, tb, :], m8[:, tb * 8:(tb + 1) * 8], lg[:, tb * 8:(tb + 1) * 8])
                E.link(i)
                E.link(e.tensor_copy(ixf.rearrange("p (t n) -> p t n", t=TB), idx[:, :, :]))
                m3 = m8.rearrange("p (t n) -> p t n", t=TB)
                x3 = ixf.rearrange("p (t n) -> p t n", t=TB)
                io = iota8.unsqueeze(1).to_broadcast([P, TB, 8])
                v3 = lambda a: a.rearrange("p (t n) -> p t n", t=TB)
                e.tensor_tensor(v3(oh0), io, x3[:, :, 0:1].to_broadcast([P, TB, 8]), ALU.is_equal)
                e.tensor_tensor(v3(oh1), io, x3[:, :, 1:2].to_broadcast([P, TB, 8]), ALU.is_equal)
                e.tensor_tensor(dv.unsqueeze(2), m3[:, :, 1:2], m3[:, :, 0:1], ALU.subtract).then_inc(top_done, 1)
                e.wait_ge(exp_done, 1)
                E.link(e.tensor_scalar(w1, ev, 1.0, None, ALU.add))
                E.link(e.reciprocal(w0, w1))
                E.link(e.tensor_tensor(w1, w0, ev, ALU.mult))
                e.tensor_tensor(v3(CW), v3(oh0), w0.unsqueeze(2).to_broadcast([P, TB, 8]), ALU.mult)
                E.link(e.tensor_tensor(v3(tmp8), v3(oh1), w1.unsqueeze(2).to_broadcast([P, TB, 8]), ALU.mult))
                E.link(e.tensor_tensor(CW, CW, tmp8, ALU.add))
                e.tensor_tensor(MSK, oh0, oh1, ALU.add).then_inc(route, 1)
            if E.kind == "act":
                e.wait_ge(top_done, 1)
                nc.scalar.activation(ev, dv, ACT.Exp).then_inc(exp_done, 1)
            if E.kind == "pe":
                e.wait_ge(route, 1)
                e.matmul(bank[2][:, 0:8], tri[:, :], MSK[:, 0:8], start=True, stop=True)
                e.matmul(bank[2][:, 8:16], ones[:, :], MSK[:, 0:8], start=True, stop=False)
                e.matmul(bank[2][:, 8:16], tri[:, :], MSK[:, 8:16], start=False, stop=True)
                e.matmul(bank[2][:, 16:24], ones[:, :], MSK[:, 0:8], start=True, stop=False)
                e.matmul(bank[2][:, 16:24], ones[:, :], MSK[:, 8:16], start=False, stop=True).then_inc(pos_full, 1)
            if E.kind == "dve":
                e.wait_ge(pos_full, 1)
                E.link(e.tensor_scalar(POS, bank[2][:, 0:16], 1.0, None, ALU.add))
                E.link(e.tensor_tensor(POS, POS, MSK, ALU.mult))
                E.link(e.tensor_scalar(POS, POS, -1.0, None, ALU.add))
                E.link(e.tensor_reduce(cntm[:, 0:1], bank[2][:, 16:24], AX.X, ALU.max))
                E.link(e.tensor_scalar(cntm[:, 1:2], cntm[:, 0:1], float(P) + 0.5, None, ALU.is_gt))
                E.link(e.tensor_copy(flag[:, 0:1], cntm[:, 1:2]))
                e.tensor_scalar(ACC[:, :, :], X[:, :, :], ALPHA, None, ALU.mult).then_inc(plan_done, 1)
            E.st.s = MOE_AT
            experts(E, 0)
            if E.kind in ("pe", "act", "dve"):
                e.wait_ge(plan_done, 1)
                over = e.value_load(flag[0:1, 0:1], min_val=0, max_val=1)
                with e.If(over > 0):
                    experts(E, 1)

        def experts(E, part):
            e = E.e
            s0 = E.st.s
            E.st.s = MOE_AT
            n0 = part * NE
            pe0 = part * (NE * H_EXP // PERIOD)
            with e.Fori(0, NE) as x:
                E.st.s = MOE_AT
                E.st.periods = x * (H_EXP // PERIOD) + pe0
                E.limit = MOE_AT + H_EXP
                E.ff.enter(x, FFE // FC)
                n = x + (n0 + 1)
                if E.kind == "act":
                    E.prologue()
                if E.kind == "dve":
                    if part == 0:
                        e.wait_ge(plan_done, 1)
                    for tb in range(TB):
                        pos = POS[:, tb * 8:(tb + 1) * 8][:, bass.ds(x, 1)]
                        cw = CW[:, tb * 8:(tb + 1) * 8][:, bass.ds(x, 1)]
                        io = iota[:, part * P:(part + 1) * P]
                        e.tensor_scalar(SE[:, tb, :], io, pos, None, ALU.is_equal)
                        i = e.tensor_scalar(SW[:, tb, :], io, pos, cw, ALU.is_equal, ALU.mult)
                    i.then_inc(se_ready, 1)
                    E.prologue()
                if E.kind == "pe":
                    e.wait_ge(se_ready, n)
                    for c in range(2):
                        for j in range(4):
                            k = 4 * c + j
                            for tb in range(TB):
                                i = e.matmul(bank[c][:, j * P:(j + 1) * P], X[:, tb, k * P:(k + 1) * P],
                                             SE[:, tb, :], start=tb == 0, stop=tb == TB - 1)
                    for tb in range(TB):
                        i = e.transpose(bank[2][:, tb * P:(tb + 1) * P], SW[:, tb, :], ident[:, :])
                    i.then_inc(xe_full, 1)
                    e.wait_ge(xe_lo, n)
                if E.kind == "act":
                    e.wait_ge(xe_full, n)
                    for c in range(2):
                        i = nc.scalar.copy(x_hi[:, 4 * c:4 * c + 4, 0:P], bank[c][:, :].rearrange(
                            "p (k n) -> p k n", n=P))
                    i.then_inc(xe_hi, 1)
                    nc.scalar.copy(SWT[:, :], bank[2][:, 0:S]).then_inc(swt_ready, 1)
                if E.kind == "dve":
                    e.wait_ge(xe_hi, n)
                    for c in range(2):
                        i = e.tensor_tensor(x_lo[:, 4 * c:4 * c + 4, 0:P], bank[c][:, :].rearrange(
                            "p (k n) -> p k n", n=P), x_hi[:, 4 * c:4 * c + 4, 0:P].bitcast(F32), ALU.subtract)
                    i.then_inc(xe_lo, 1)
                ffn(E, FFE // FC, 1)
                if E.kind == "act":
                    e.wait_ge(w_used, E.st.done(-1))
                    for c in range(2):
                        i = nc.scalar.copy(YE[:, c * 512:(c + 1) * 512], bank[4 + c][:, :])
                    i.then_inc(ye_ready, 1)
                if E.kind == "pe":
                    e.wait_ge(ye_ready, n)
                    for tb in range(TB):
                        for c in range(2):
                            i = e.matmul(bank[4 + 2 * tb + c][:, :], SWT[:, tb * P:(tb + 1) * P],
                                         YE[:, c * 512:(c + 1) * 512], start=True, stop=True)
                    i.then_inc(sc_full, 1)
                if E.kind == "dve":
                    e.wait_ge(sc_full, n)
                    for tb in range(TB):
                        for c in range(2):
                            a = ACC[:, tb, c * 512:(c + 1) * 512]
                            i = e.tensor_tensor(a, a, bank[4 + 2 * tb + c][:, :], ALU.add)
                    i.then_inc(sc_done, 1)
                    e.wait_ge(sc_done, n)
                if E.kind == "pe":
                    e.wait_ge(sc_done, n)
                E.ff.leave(NE)
            E.st.periods = 0
            E.st.s = s0

        def program(E):
            e = E.e
            if E.kind == "act":
                e.wait_ge(c_in, N_CONST * 16)
            if E.kind == "dve":
                e.memset(half_c, -0.5).then_inc(half_set, 1)
                e.wait_ge(half_set, 1)
                e.wait_ge(c_in, N_CONST * 16)
                e.wait_ge(x_in, 16)
                E.link(e.memset(ms, 1.0))
            if E.kind == "pe":
                e.wait_ge(c_in, N_CONST * 16)
            if E.kind == "pool":
                e.wait_ge(half_set, 1)
            E.prologue()
            for l in range(LAYERS):
                pool_tables(E, l)
                first_layer(E, l)
            pool_ln(E, 0)
            layer_norm(E)
            for l in range(LAYERS):
                pool_ln(E, 1 + 2 * l)
                pool_mixer(E, l)
                second_mixer(E, l)
                pool_ln(E, 2 + 2 * l)
                if l == 0:
                    if E.kind == "dve":
                        e.engine_nop().then_inc(tp_src, 1)
                    tp_stage(E, X, KD, 0)
                    if E.kind == "pe":
                        e.wait_ge(tp_lo, E.tp.at())
                    ffn(E, FF1 // FC, TB)
                    residual(E)
                else:
                    moe(E)
                    if E.kind == "dve":
                        E.link(e.tensor_copy(X[:, :, :], ACC[:, :, :]))
                layer_norm(E)
            if E.kind == "dve":
                e.engine_nop().then_inc(x_final, 1)

        def pool_tables(E, l):
            if E.kind == "pool":
                e = E.e
                if l:
                    e.wait_ge(h_ready, l * (FF1 // FC))
                e.dma_start(CT, A["ropec"].rearrange("(t p) n -> p t n", p=P)).then_inc(tab_in, 16)
                e.dma_start(ST, A["ropes"].rearrange("(t p) n -> p t n", p=P)).then_inc(tab_in, 16)
                e.dma_start(rowv, A["rowv"][l:l + 1, :].to_broadcast([P, ROWV])).then_inc(tab_in, 16)

        def pool_ln(E, n):
            if E.kind == "pool":
                e = E.e
                if n == 0:
                    e.wait_ge(h_ready, LAYERS * (FF1 // FC))
                else:
                    e.wait_ge(ln_done, n)
                e.dma_start(GB, A["lngb"][n:n + 1, :].to_broadcast([P, 2 * D])).then_inc(lnb_in, 16)

        def pool_mixer(E, l):
            if E.kind != "pool":
                return
            e = E.e
            if l:
                e.wait_ge(o_done, LAYERS * N_MAP1 + l * N_MAP2)
                e.wait_ge(h_ready, (LAYERS + l) * (FF1 // FC))
            e.dma_start(BG, A["bgate"][l:l + 1, 0:D].to_broadcast([P, D])).then_inc(bg_in, 16)
            e.dma_start(BG2, A["bgate"][l:l + 1, D:2 * D].to_broadcast([P, D])).then_inc(bg_in, 16)
            e.dma_start(BT[:, NBT - 1], A["band"].rearrange("(t p) n -> p t n", p=P)).then_inc(bg_in, 16)
            e.dma_start(sinkb, A["sink"][l:l + 1, :].to_broadcast([P, SH])).then_inc(bg_in, 16)
            if l == 0:
                e.dma_start(T2[:, 0:KD * NE], A["router"]).then_inc(bt_in[2], 16)
            for h in range(NH):
                slot = h % 2
                if h >= 2:
                    e.wait_ge(mx_done, LAYERS * N_MAP1 + l * N_MAP2 + h - 1)
                for tb in range(TB):
                    for r in range(2):
                        row = 2 * tb + r
                        e.dma_start(BT[r * 64:(r + 1) * 64, slot, tb, :],
                                    A["rpb"][l, h, :, (ROWS - 1 - row) * GRID_W:(2 * ROWS - 1 - row) * GRID_W]
                                    ).then_inc(bt_in[slot], 16)
                e.wait_ge(bt_in[slot], 64 * (l * NH // 2 + h // 2 + 1))
                b = BT[:, slot].rearrange("p t (r n) -> p (t r) n", n=GRID_W)
                e.tensor_tensor(b, b, namask[:, :].unsqueeze(1).to_broadcast([P, TB * ROWS, GRID_W]),
                                ALU.add).then_inc(bt_ready, 1)

        consts = [(ident[:, :], "ident"), (iota[:, :], "iota"), (tri[:, :], "tri"), (ones[:, :], "ones"),
                  (namask[:, :], "namask"), (colg[:, :, :], "colg"), (iota8, "iota8"),
                  (rotc.rearrange("p (t n) -> p t n", t=TB), "rotc"), (rots.rearrange("p (t n) -> p t n", t=TB), "rots")]
        N_CONST = len(consts)

        block = ctx.enter_context(nc.Block())

        @block.sync
        def _(sp):
            sp.dma_start(X[:, :, :], A["x"].rearrange("(t p) n -> p t n", p=P)).then_inc(x_in, 16)
            for dst, name in consts:
                src = A[name]
                if name in ("rotc", "rots"):
                    src = src.rearrange("(t p) n -> p t n", p=P)
                sp.dma_start(dst, src).then_inc(c_in, 16)
            stream = A["stream"]

            def load(slot, group, used, free):
                wait(sp, lo_done, free)
                src = stream[group] if isinstance(group, int) else stream[group].rearrange("o p n -> (o p) n")
                sp.dma_start(raw[:, slot, :], src).then_inc(raw_in[slot], 16)
            groups = TOTAL // 2
            for g in range(RAW):
                load(g, g, 0, 0)
            rounds = groups // RAW - 1
            with sp.Fori(0, rounds) as i:
                for s in range(RAW):
                    load(s, bass.ds(i * RAW + (RAW + s), 1), 0, i * PERIOD + (2 * s + 2))
            for g in range(RAW * (rounds + 1), groups):
                load(g % RAW, g, 0, 2 * (g - RAW) + 2)
            sp.wait_ge(plan_done, 1)
            over = sp.value_load(flag[0:1, 0:1], min_val=0, max_val=1)
            with sp.If(over > 0):
                first = MOE_AT // 2
                n = groups - first
                with sp.Fori(0, n // RAW) as i:
                    for s in range(RAW):
                        slot = (groups + s) % RAW
                        load(slot, bass.ds(i * RAW + (first + s), 1), 0,
                             i * PERIOD + (2 * (groups + s - RAW) + 2))
            sp.wait_ge(x_final, 1)
            sp.dma_start(A["out"].rearrange("(t p) n -> p t n", p=P), X[:, :, :]).then_inc(out_done, 16)
            sp.wait_ge(out_done, 16)

        @block.tensor
        def _(pe):
            program(Eng(pe, "pe"))

        @block.scalar
        def _(act):
            program(Eng(act, "act"))

        @block.vector
        def _(dve):
            program(Eng(dve, "dve"))

        @block.gpsimd
        def _(pool):
            program(Eng(pool, "pool"))


def _halves_cols(w, width):
    k = w.shape[0] // P
    n = w.shape[1]
    per = 4 if n == 256 else 2
    stride = HALF // per
    b = np.zeros((k // per, P, per, stride), np.float32)
    b[..., :n] = w.reshape(k // per, per, P, n).transpose(0, 2, 1, 3)
    return b.reshape(k // per, P, HALF)


def _halves_rows(w):
    k, n = w.shape[0] // P, w.shape[1]
    b = np.zeros((k, P, HALF), np.float32)
    b[:, :, :n] = w.reshape(k, P, n)
    return b


def _ffn(wg, wu, wd):
    n = wg.shape[1] // FC

    def gu(c):
        s = slice(c * FC, (c + 1) * FC)
        return _halves_cols(np.concatenate([wg[:, s], wu[:, s]], 1), 512)

    def dn(c):
        return _halves_rows(wd[c * FC:(c + 1) * FC])
    out = [gu(0)]
    for c in range(1, n):
        out += [gu(c), dn(c - 1)]
    return out + [dn(n - 1)]


def _pair(w, c, kv, group):
    w = w.copy()
    n = kv * group * 64
    w[:, c:c + n] = w[:, c:c + n].reshape(-1, kv, group, 64).transpose(0, 2, 1, 3).reshape(-1, n)
    return w


def _swap(g, parts):
    g = g.copy()
    for a, w in parts:
        h = w // 2
        g[..., a:a + h], g[..., a + h:a + w] = g[..., a + h:a + w].copy(), g[..., a:a + h].copy()
    return g


def _cos_sin(pos, dim, theta):
    inv = 1.0 / (theta ** (np.arange(0, dim, 2, dtype=np.float32) / np.float32(dim)))
    ang = pos.astype(np.float32)[:, None] * inv.astype(np.float32)[None, :]
    return np.cos(ang, dtype=np.float32), np.sin(ang, dtype=np.float32)


def _layout(a):
    f = lambda n: np.asarray(a[n])
    out = {"x": f("x").reshape(S, D)}
    parts = []
    for l in range(LAYERS):
        w = _pair(f("w_in")[l], C_GQ, GKV, GH // GKV)
        parts += [_halves_cols(w[:, c:c + n], n) for c, n in chunks_in1()]
        parts += [_halves_rows(f("mla_w_uq")[l]), _halves_rows(f("mla_w_ukv")[l]), _halves_rows(f("w_o")[l])]
        g = f("w_gate_up")[l]
        parts += _ffn(g[:, :FF1], g[:, FF1:], f("w_down")[l])
    for l in range(LAYERS):
        w = _pair(f("w_in_2")[l], C_QS, SKV, SH // SKV)
        parts += [_halves_cols(w[:, c:c + n], n) for c, n in chunks_in2()]
        parts += [_halves_rows(f(n)[l]) for n in ("w_branch_na_2", "w_branch_sw_2", "w_out_2")]
        if l == 0:
            parts += _ffn(f("ffn_w_gate_2")[0], f("ffn_w_up_2")[0], f("ffn_w_down_2")[0])
        else:
            for x in range(NE):
                parts += _ffn(f("moe_w_gate_2")[0, x], f("moe_w_up_2")[0, x], f("moe_w_down_2")[0, x])
    s = np.concatenate(parts, 0)
    assert s.shape[0] == TOTAL, (s.shape, TOTAL)
    out["stream"] = np.ascontiguousarray(s.reshape(TOTAL // 2, 2, P, HALF).transpose(0, 2, 1, 3)).reshape(
        TOTAL // 2, P, GROUP)
    col = [f(n).reshape(LAYERS, -1, P) for n in ("attn_norm", "ffn_norm", "mla_q_norm", "mla_kv_norm")]
    out["colg"] = np.ascontiguousarray(np.concatenate(col, 1).transpose(2, 0, 1))
    g = [f(n) for n in ("mla_q_gain", "mla_k_gain", "diff_q_gain", "diff_k_gain", "gqa_q_gain", "gqa_k_gain")]
    ax = [(0, GD // 2), (GD // 2, GD // 2)]
    rot = [[(MNOPE, MROPE)]] * 2 + [[(0, DQ)]] * 2 + [ax] * 2
    out["rowv"] = np.concatenate(g + [_swap(x, r) for x, r in zip(g, rot)] + [f("diff_out_gain")] + [
        f(n) for n in ("diff_lq1", "diff_lk1", "diff_lq2", "diff_lk2")], 1)
    pos = np.arange(S)
    cm, snm = _cos_sin(pos, MROPE, 10000.0)
    cd, sd = _cos_sin(pos, DQ, 10000.0)
    cr, sr = _cos_sin(pos // GRID_W, GD // 2, 10000.0)
    cc, sc = _cos_sin(pos % GRID_W, GD // 2, 10000.0)
    one, zero = np.ones((S, MNOPE), np.float32), np.zeros((S, MNOPE), np.float32)
    mc, msn = [one, cm, cm], [zero, -snm, snm]
    gc, gs = [cr, cr, cc, cc], [-sr, sr, -sc, sc]
    out["ropec"] = np.concatenate(mc * 2 + [cd, cd] * 2 + gc * 2, 1)
    out["ropes"] = np.concatenate(msn * 2 + [-sd, sd] * 2 + gs * 2, 1)
    c2, s2 = _cos_sin(pos, ROT, 500000.0)
    out["rotc"], out["rots"] = np.concatenate([c2, c2], 1), np.concatenate([-s2, s2], 1)
    lng = np.stack([f("emb_ln_g_2"), f("ln1_g_2")[0], f("ln2_g_2")[0], f("ln1_g_2")[1], f("ln2_g_2")[1]])
    lnb = np.stack([f("emb_ln_b_2"), f("ln1_b_2")[0], f("ln2_b_2")[0], f("ln1_b_2")[1], f("ln2_b_2")[1]])
    out["lngb"] = np.concatenate([lng, lnb], 1)
    out["bgate"], out["sink"] = f("b_gate_2"), f("sw_sink_2")
    out["router"] = np.ascontiguousarray(f("moe_router_2")[0].reshape(KD, P, NE).transpose(1, 0, 2)).reshape(P, KD * NE)
    r = f("na_rpb_2")
    kw = r.shape[3] // 2
    rows = r[:, :, r.shape[2] // 2 - ROWS + 1:r.shape[2] // 2 + ROWS]
    pad = np.zeros(rows.shape[:3] + (2 * GRID_W - 1,), np.float32)
    pad[..., GRID_W - 1 - kw:GRID_W + kw] = rows
    q, k = np.arange(GRID_W)[:, None], np.arange(GRID_W)[None, :]
    out["rpb"] = np.ascontiguousarray(pad[..., k - q + GRID_W - 1].transpose(0, 1, 3, 2, 4)).reshape(
        LAYERS, NH, GRID_W, -1)
    half = (kw + 1) // 2
    first = np.clip(q - half, 0, GRID_W - 2 * half)
    m = np.where((k >= first) & (k < first + 2 * half), 0.0, NEG).astype(np.float32)
    out["namask"] = np.concatenate([m, m], 0)
    t = np.arange(S)
    out["band"] = np.where(np.abs(t[:, None] - t[None, :]) <= 128, 0.0, NEG).astype(np.float32)
    out["ident"] = np.eye(P, dtype=np.float32)
    out["iota"] = np.broadcast_to(t.astype(np.float32), (P, S))
    out["iota8"] = np.broadcast_to(np.arange(NE, dtype=np.float32), (P, NE))
    out["tri"] = np.triu(np.ones((P, P), np.float32), 1)
    out["ones"] = np.ones((P, P), np.float32)
    return {n: np.ascontiguousarray(v) for n, v in out.items()}


def kernel(**inputs):
    import concourse.bacc as _bacc
    from concourse.bass_utils import run_bass_kernel_spmd as _run

    arrays = _layout(inputs)
    nc = _bacc.Bacc("TRN2", target_bir_lowering=False, num_devices=1)
    A = {n: nc.dram_tensor("in_" + n, v.shape, mybir.dt.from_np(v.dtype), kind="ExternalInput").ap()
         for n, v in arrays.items()}
    A["out"] = nc.dram_tensor("out_y", (S, D), F32, kind="ExternalOutput").ap()
    build(nc, A)
    r = _run(nc, [{"in_" + n: v for n, v in arrays.items()}], core_ids=[0])
    return r.results[0]["out_y"].reshape(1, S, D)
```

```python
import math
from contextlib import ExitStack

import numpy as np

import concourse.bass as bass
from concourse import mybir

F32 = mybir.dt.float32
F32R = mybir.dt.float32r
I32 = mybir.dt.int32
U32 = mybir.dt.uint32
ALU = mybir.AluOpType
ACT = mybir.ActivationFunctionType
AX = mybir.AxisListType

P = 128
S = 256
TB = S // P
D = 1024
KD = D // P
LAYERS = 2
EPS = 1e-6
SMALL = 720
XW = 12
LN_EPS = 1e-5
ALPHA = (2 * LAYERS) ** 0.25

MH, MQR, MKVR, MNOPE, MROPE, MV = 6, 384, 256, 64, 32, 64
MQK = MNOPE + MROPE
DH, DQ = 4, 64
DV = 2 * DQ
GH, GKV, GD = 6, 2, 64
C_CQ, C_CKV = 0, MQR
C_KR = C_CKV + MKVR
C_DQ = C_KR + MROPE
C_DK = C_DQ + 2 * DH * DQ
C_GQ = C_DK + 2 * DH * DQ
C_GK = C_GQ + GH * GD
C_GV = C_GK + GKV * GD
C_DV = C_GV + GKV * GD
W_IN1 = C_DV + DH * DV
MIX = MH * MV + DH * DV + GH * GD
FF1 = 2816

HD = 64
NH, SH, SKV = 8, 8, 2
W_NA = NH * HD
W_QKV2 = 3 * W_NA + SH * HD + 2 * SKV * HD
C_QS = 3 * W_NA
C_KS = C_QS + SH * HD
C_VS = C_KS + SKV * HD
ROT = HD // 4
GRID_W = 64
ROWS = S // GRID_W
NE = 8
FFE = 3584
NEG = -1e30

GROUP = 2048
HALF = GROUP // 2
RAW = 6
SPLIT = 4
AHEAD = SPLIT - 1
PERIOD = 2 * RAW
FC = 256


def chunks_in1():
    return [(c, min(512, W_IN1 - c)) for c in range(0, W_IN1, 512)]


def chunks_in2():
    return [(c, min(512, W_QKV2 - c)) for c in range(0, W_QKV2, 512)] + [
        (W_QKV2 + c, 512) for c in range(0, 2 * D, 512)]


def halves_of(width):
    return 2 if width == 256 else 4


H_IN1 = sum(halves_of(w) for _, w in chunks_in1())
H_UQ, H_UKV, H_O = MQR // P, MKVR // P, MIX // P
H_FF1 = FF1 // FC * 6
H_L1 = H_IN1 + H_UQ + H_UKV + H_O + H_FF1
H_MIX2 = sum(halves_of(w) for _, w in chunks_in2()) + 2 * (W_NA // P) + D // P
H_EXP = FFE // FC * 6
H_DENSE = LAYERS * H_L1 + 2 * H_MIX2 + H_FF1
MOE_AT = H_DENSE
TOTAL = MOE_AT + NE * H_EXP
assert H_EXP % PERIOD == 0 and MOE_AT % 2 == 0
SOURCES = 2 * LAYERS * 6 + 2
LEAD = -(-AHEAD // 2)

A_H = 0
A_QA = A_H + TB * W_IN1
A_KV = A_QA + TB * MH * MQK
A_KA = A_KV + TB * MH * (MNOPE + MV)
A_MLA = A_KA + TB * MH * MQK
A_T3 = A_MLA + TB * MH * (MQK + MROPE)
A_END = A_T3 + TB * DV
N_QK1 = 2 * DH + GH // GKV + 1
N_QK = N_QK1 + 2 * MH - 2 * DH
B_H = 0
B_G = B_H + TB * W_QKV2
B_SS = B_G + TB * 2 * D
N_QK2 = NH + SH // SKV + 1
assert N_QK2 <= N_QK
N_MAP1 = 2 * DH + GH + MH
N_MAP2 = NH + SH
B_BT = B_SS + 2 * TB * S
NBT = 5
B_T = B_BT + NBT * TB * S
E_SIL = 0
E_HH = E_SIL + TB * FC
E_S = E_HH + TB * FC
E_SW = E_S + TB * P
E_SWT = E_SW + TB * P
E_YE = E_SWT + 2 * S

ROPEW = 2 * (MQK + DQ + GD)
F_MQ, F_MK, F_DQ, F_DK, F_GQ, F_GK = 0, MQK, 2 * MQK, 2 * MQK + DQ, 2 * MQK + 2 * DQ, 2 * MQK + 2 * DQ + GD
R_G, R_GS, R_OG, R_LAM = 0, ROPEW, 2 * ROPEW, 2 * ROPEW + DV
ROWV = R_LAM + 4 * DQ
CG_ATTN, CG_FFN, CG_Q, CG_KV = 0, KD, 2 * KD, 2 * KD + MQR // P
CGW = CG_KV + MKVR // P


class Count:

    def __init__(self):
        self.base, self.n, self.saved = 0, 0, []

    def at(self, d=0):
        return self.base + (self.n + d)

    def enter(self, i, per):
        self.saved.append((self.base, self.n, per))
        self.base = self.base + (i * per + self.n)
        self.n = 0

    def leave(self, trips):
        base, n, per = self.saved.pop()
        assert self.n == per, (self.n, per)
        self.base, self.n = base, n + trips * per


def wait(e, sem, value):
    if not isinstance(value, int) or value > 0:
        e.wait_ge(sem, value)


class Stream:

    def __init__(self):
        self.s, self.periods = 0, 0

    def half(self, d=0):
        s = self.s + d
        return s, self.periods

    def done(self, d=0):
        return self.periods * PERIOD + (self.s + d + 1)


def build(nc, A):
    ctx = ExitStack()
    with ctx:
        def sb(name, shape, dt=F32):
            return ctx.enter_context(nc.sbuf_tensor(name, shape, dt))

        def sem(name):
            return ctx.enter_context(nc.semaphore(name))

        raw = sb("raw", [P, RAW, GROUP])
        w_hi = sb("w_hi", [P, SPLIT, HALF], F32R)
        w_lo = sb("w_lo", [P, SPLIT, HALF], F32R)
        X = sb("X", [P, TB, D])
        KX = MIX // P
        x_hi = sb("x_hi", [P, KX, S], F32R)
        x_lo = sb("x_lo", [P, KX, S], F32R)
        O = sb("O", [P, TB, MIX])
        arena = sb("arena", [P, max(A_END, B_T)])
        qk_t = sb("qk_t", [P, N_QK, S], F32R)
        PP = sb("PP", [P, 2, TB, S])
        PT = sb("PT", [P, 2, TB, S])
        tab = sb("tab", [P, 2 * TB * ROPEW + ROWV])
        small = sb("small", [P, SMALL])
        ident = sb("ident", [P, P])
        colg = sb("colg", [P, LAYERS, CGW])
        rw_hi = sb("rw_hi", [P, KD, NE], F32R)
        rw_lo = sb("rw_lo", [P, KD, NE], F32R)
        flag = sb("flag", [P, 8], I32)
        idx = sb("idx", [P, TB, 8], U32)
        bank = [ctx.enter_context(nc.psum_tensor(f"bank{i}", [P, 512], F32)) for i in range(8)]

        XS = O[:, :, 0:D]
        H = arena[:, A_H:A_QA].rearrange("p (t n) -> p t n", t=TB)
        QA = arena[:, A_QA:A_KV].rearrange("p (t n) -> p t n", t=TB)
        KV = arena[:, A_KV:A_KA].rearrange("p (t n) -> p t n", t=TB)
        KA = arena[:, A_KA:A_MLA].rearrange("p (t n) -> p t n", t=TB)
        H2 = arena[:, B_H:B_G].rearrange("p (t n) -> p t n", t=TB)
        G2 = arena[:, B_G:B_SS].rearrange("p (t n) -> p t n", t=TB)
        SS = arena[:, B_SS:B_BT].rearrange("p (b t n) -> p b t n", b=2, t=TB)
        BT = arena[:, B_BT:B_T].rearrange("p (b t n) -> p b t n", b=NBT, t=TB)
        junk = arena[:, B_G:B_G + TB * D].rearrange("p (t n) -> p t n", t=TB)
        YG = arena[:, B_H:B_H + TB * D].rearrange("p (t n) -> p t n", t=TB)
        SIL = arena[:, E_SIL:E_HH].rearrange("p (t n) -> p t n", t=TB)
        HH = arena[:, E_HH:E_S].rearrange("p (t n) -> p t n", t=TB)
        SE = arena[:, E_S:E_SW].rearrange("p (t n) -> p t n", t=TB)
        SW = arena[:, E_SW:E_SWT].rearrange("p (t n) -> p t n", t=TB)
        SWT = arena[:, E_SWT:E_YE].rearrange("p (b n) -> p b n", b=2)
        sum_bank = [bank[1], bank[3], bank[6], bank[7]]
        YE = arena[:, E_YE:E_YE + D]
        CT = tab[:, 0:TB * ROPEW].rearrange("p (t n) -> p t n", t=TB)
        ST = tab[:, TB * ROPEW:2 * TB * ROPEW].rearrange("p (t n) -> p t n", t=TB)
        rowv = tab[:, 2 * TB * ROPEW:]
        GB = tab[:, 0:2 * D]
        BG = PP[:, :, :, :].rearrange("p b t n -> p (b t n)")
        BG2 = PT[:, :, :, :].rearrange("p b t n -> p (b t n)")
        t1, t2 = BG, BG2
        sc_mla = arena[:, A_MLA:A_T3]
        t3 = arena[:, A_T3:A_END]
        hT_hi, hT_lo = x_hi[:, KD:KD + 2, :], x_lo[:, KD:KD + 2, :]

        at = [0]

        def sm(n):
            at[0] += n
            assert at[0] <= SMALL
            return small[:, at[0] - n:at[0]]

        half_c = sm(64)
        ms, rs = sm(64), sm(64)
        ssx, ssk = sm(2), sm(2)
        mx, negm, psum_, rsum, esink = sm(8), sm(8), sm(8), sm(8), sm(8)
        lamv, lame, nlam = sm(2), sm(2), sm(1)
        sinkb = sm(8)
        sx, negmu, msx, rsx = sm(4), sm(2), sm(2), sm(2)
        rotc, rots = sm(TB * ROT), sm(TB * ROT)
        lg, m8, ixf = sm(16), sm(16), sm(16)
        dv, ev, w0, w1 = sm(2), sm(2), sm(2), sm(2)
        CW, POS = sm(2 * XW), sm(2 * XW)
        MSK = sm(16)
        oh0, oh1, tmp8 = sm(16), sm(16), sm(16)
        cntm = sm(8)
        kr1, kr2 = sm(TB * MROPE), sm(TB * MROPE)
        iota8 = sm(8)
        iota = sb("iota", [P, S])
        tri, ones = tab[:, 2 * D:2 * D + P], tab[:, 2 * D + P:2 * D + 2 * P]
        router = sb("router", [P, KD, NE])

        raw_in = [sem(f"raw_in{i}") for i in range(RAW)]
        hi_done = sem("hi_done")
        lo_done = sem("lo_done")
        w_used = sem("w_used")
        c_in = sem("c_in")
        x_in = sem("x_in")
        tab_in = sem("tab_in")
        lnb_in = sem("lnb_in")
        bg_in = sem("bg_in")
        bt_in = [sem(f"bt_in{i}") for i in range(NBT - 1)]
        route_in = sem("route_in")
        out_done = sem("out_done")
        half_set = sem("half_set")
        dve_step = sem("dve_step")
        ms_ready = sem("ms_ready")
        rs_ready = sem("rs_ready")
        sq_done = sem("sq_done")
        msx_done = sem("msx_done")
        xr_ready = sem("xr_ready")
        mu_ready = sem("mu_ready")
        tp_src = sem("tp_src")
        tp_full = sem("tp_full")
        tp_hi = sem("tp_hi")
        tp_lo = sem("tp_lo")
        acc_act = sem("acc_act")
        acc_dve = sem("acc_dve")
        qk_src = sem("qk_src")
        qk_full = sem("qk_full")
        qk_hi = sem("qk_hi")
        qk_lo = sem("qk_lo")
        s_full = sem("s_full")
        mx_done = sem("mx_done")
        p_ready = sem("p_ready")
        pt_full = sem("pt_full")
        pt_act = sem("pt_act")
        pt_dve = sem("pt_dve")
        o_full = sem("o_full")
        o_done = sem("o_done")
        lam_sum, lam_exp = sem("lam_sum"), sem("lam_exp")
        sil_done = sem("sil_done")
        h_ready = sem("h_ready")
        ht_full = sem("ht_full")
        ht_hi = sem("ht_hi")
        ht_lo = sem("ht_lo")
        rw_split = sem("rw_split")
        lg_full = sem("lg_full")
        top_done = sem("top_done")
        exp_done = sem("exp_done")
        route = sem("route")
        pos_full = sem("pos_full")
        plan_done = sem("plan_done")
        se_ready = sem("se_ready")
        xe_full = sem("xe_full")
        xe_hi = sem("xe_hi")
        xe_lo = sem("xe_lo")
        ye_zero = sem("ye_zero")
        ye_ready = sem("ye_ready")
        sc_full = sem("sc_full")

        def split_hi(e, st, d):
            s, n = st.half(d)
            slot = s // 2 % RAW
            if s % 2 == 0:
                e.wait_ge(raw_in[slot], (n + (s // PERIOD + 1)) * 16)
            wait(e, w_used, st.done(d) - SPLIT)
            nc.scalar.copy(w_hi[:, s % SPLIT, :], raw[:, slot, s % 2 * HALF:(s % 2 + 1) * HALF]).then_inc(hi_done, 1)

        def split_lo(e, st, d):
            s, n = st.half(d)
            slot = s // 2 % RAW
            e.wait_ge(hi_done, st.done(d))
            e.tensor_tensor(w_lo[:, s % SPLIT, :], raw[:, slot, s % 2 * HALF:(s % 2 + 1) * HALF],
                            w_hi[:, s % SPLIT, :].bitcast(F32), ALU.subtract).then_inc(lo_done, 1)

        class Eng:

            def __init__(self, e, kind):
                self.e, self.kind = e, kind
                self.st = Stream()
                self.src, self.tp = Count(), Count()
                self.acc = Count()
                self.rs = Count()
                self.xr = Count()
                self.pairs = 0
                self.qks, self.qk = Count(), Count()
                self.map = Count()
                self.ff = Count()
                self.ln = Count()
                self.chain = Count()

            def link(self, ins):
                ins.then_inc(dve_step, 1)
                self.chain.n += 1
                self.e.wait_ge(dve_step, self.chain.at())

            def half_step(self, use=None):
                if self.kind == "pe":
                    s, _ = self.st.half()
                    self.e.wait_ge(lo_done, self.st.done())
                    use(w_hi[:, s % SPLIT, :], w_lo[:, s % SPLIT, :]).then_inc(w_used, 1)
                elif self.kind == "act":
                    split_hi(self.e, self.st, AHEAD)
                elif self.kind == "dve":
                    split_lo(self.e, self.st, AHEAD)
                self.st.s += 1

            def prologue(self):
                for d in range(AHEAD):
                    if self.kind == "act":
                        split_hi(self.e, self.st, d)
                    elif self.kind == "dve":
                        split_lo(self.e, self.st, d)

        def mm3(pe, out, xh, xl, wh, wl, first, last):
            pe.matmul(out, xh, wh, start=first, stop=False)
            pe.matmul(out, xh, wl, start=False, stop=False)
            return pe.matmul(out, xl, wh, start=False, stop=last)

        def tp_stage(E, src, blocks, k0, gain=None, parts=1, t_bank=4):
            e = E.e
            E.pairs = (blocks + 1) // 2
            for b0 in range(0, blocks, 2):
                nb = min(2, blocks - b0)
                if E.kind == "pe":
                    e.wait_ge(tp_src, E.src.at(1 + b0 * parts // blocks))
                pb = bank[t_bank + E.tp.n % 4][:, 0:nb * S]
                if E.kind == "pe":
                    wait(e, tp_lo, E.tp.at(1 - 4))
                    for b in range(nb):
                        for tb in range(TB):
                            i = e.transpose(pb[:, b * S + tb * P:b * S + (tb + 1) * P],
                                            src[:, tb, (b0 + b) * P:(b0 + b + 1) * P], ident[:, :])
                    i.then_inc(tp_full, 1)
                elif E.kind == "act":
                    e.wait_ge(tp_full, E.tp.at(1))
                    if gain is None:
                        i = nc.scalar.copy(x_hi[:, k0 + b0:k0 + b0 + nb, :], pb.rearrange("p (b n) -> p b n", n=S))
                    else:
                        for b in range(nb):
                            i = nc.scalar.activation(x_hi[:, k0 + b0 + b, :], pb[:, b * S:(b + 1) * S], ACT.Copy,
                                                     scale=gain[:, b0 + b:b0 + b + 1])
                    i.then_inc(tp_hi, 1)
                elif E.kind == "dve":
                    e.wait_ge(tp_hi, E.tp.at(1))
                    if gain is None:
                        i = e.tensor_tensor(x_lo[:, k0 + b0:k0 + b0 + nb, :], pb.rearrange("p (b n) -> p b n", n=S),
                                            x_hi[:, k0 + b0:k0 + b0 + nb, :].bitcast(F32), ALU.subtract)
                    else:
                        for b in range(nb):
                            i = e.scalar_tensor_tensor(x_lo[:, k0 + b0 + b, :], pb[:, b * S:(b + 1) * S],
                                                       gain[:, b0 + b:b0 + b + 1],
                                                       x_hi[:, k0 + b0 + b, :].bitcast(F32), ALU.mult, ALU.subtract)
                    i.then_inc(tp_lo, 1)
                E.tp.n += 1
            E.src.n += parts

        def need(E, k):
            if E.kind == "pe" and k % 2 == 0:
                E.e.wait_ge(tp_lo, E.tp.at(k // 2 + 1 - E.pairs))

        def rsqrt(E, at, n):
            if E.kind == "pool":
                E.e.wait_ge(ms_ready, E.rs.at(1))
                r = slice(at, at + n)
                E.e.tensor_tensor(rs[:, r], ms[:, r], half_c[:, r], ALU.pow).then_inc(rs_ready, 1)
            E.rs.n += 1

        def need_rs(E):
            E.e.wait_ge(rs_ready, E.rs.at())

        def square_sums(E, bias=None):
            if E.kind == "act":
                for tb in range(TB):
                    if bias is None:
                        i = nc.scalar.activation(junk[:, tb, :], X[:, tb, :], ACT.Square, accum_out=ssx[:, tb:tb + 1])
                    else:
                        E.e.wait_ge(mu_ready, TB * E.ln.at() + (tb + 1))
                        i = nc.scalar.activation(junk[:, tb, :], X[:, tb, :], ACT.Square, bias=bias[:, tb:tb + 1],
                                                 accum_out=ssx[:, tb:tb + 1])
                i.then_inc(sq_done, 1)

        def row_scale(E, eps):
            if E.kind == "pool":
                e = E.e
                e.wait_ge(sq_done, E.xr.at(1))
                e.tensor_scalar(msx, ssx, 1.0 / D, eps, ALU.mult, ALU.add).then_inc(msx_done, 1)
                e.wait_ge(msx_done, E.xr.at(1))
                e.tensor_tensor(rsx, msx, half_c[:, 0:2], ALU.pow).then_inc(xr_ready, 1)
            E.xr.n += 1

        def need_scale(E):
            E.e.wait_ge(xr_ready, E.xr.at())

        def norm_transposes(E, gain, t_bank):
            tp_stage(E, X, KD, 0, gain, parts=2, t_bank=t_bank)
            square_sums(E)
            row_scale(E, EPS)

        def gemm_cols(E, width, evac_act, evac_dve, fresh=False, aside=None, kn=KD):
            e = E.e
            b = 4 + 2 * (E.acc.n % 2)
            per = HALF // width if kn == KD else 1
            nh = kn // per
            if width == 288 or width == 384:
                nh, per = kn // 2, 2
            if E.kind == "pe":
                wait(e, acc_act, E.acc.at(1 - 2))
                wait(e, acc_dve, E.acc.at(1 - 2))
            for hx in range(nh):
                if fresh:
                    need(E, hx * per)

                def use(wh, wl, hx=hx):
                    stride = HALF // per
                    for j in range(per):
                        k = hx * per + j
                        w = slice(j * stride, j * stride + width)
                        for tb in range(TB):
                            t = slice(tb * P, (tb + 1) * P)
                            i = mm3(e, bank[b + tb][:, 0:width], x_hi[:, k, t], x_lo[:, k, t], wh[:, w], wl[:, w],
                                    k == 0, k == kn - 1)
                    return i
                E.half_step(use)
                if aside:
                    aside(hx)
            if E.kind == "act":
                e.wait_ge(w_used, E.st.done(-1))
                evac_act(bank[b]).then_inc(acc_act, 1)
            if E.kind == "dve":
                e.wait_ge(w_used, E.st.done(-1))
                evac_dve(bank[b + 1]).then_inc(acc_dve, 1)
            E.acc.n += 1

        def gemm_rows(E, nh, k0, b0=0):
            e = E.e
            for hx in range(nh):
                need(E, k0 + hx)

                def use(wh, wl, hx=hx):
                    for tb in range(TB):
                        t = slice(tb * P, (tb + 1) * P)
                        for c in range(2):
                            w = slice(c * 512, (c + 1) * 512)
                            i = mm3(e, bank[b0 + 2 * tb + c][:, :], x_hi[:, k0 + hx, t], x_lo[:, k0 + hx, t],
                                    wh[:, w], wl[:, w], hx == 0, hx == nh - 1)
                    return i
                E.half_step(use)

        def scalar_rows(E, fn, b0=0):
            if E.kind == "dve":
                E.e.wait_ge(w_used, E.st.done(-1))
                for tb in range(TB):
                    for c in range(2):
                        fn(tb, c, bank[b0 + 2 * tb + c][:, :])

        def heads_view(a, n, d):
            return a.rearrange("p (t h d) -> p t h d", t=TB, h=n)

        def over_heads(tab4, n):
            return tab4.unsqueeze(2).to_broadcast([P, TB, n, tab4.shape[2]])

        def scales(at, n, d):
            return rs[:, at:at + TB * n].rearrange("p (t h) -> p t h", t=TB).unsqueeze(3).to_broadcast([P, TB, n, d])

        def head_squares(E, x, n, d, at, y):
            e = E.e
            E.link(e.tensor_tensor(heads_view(y, n, d), x, x, ALU.mult))
            E.link(e.tensor_reduce(ms[:, at:at + TB * n], y.rearrange("p (m d) -> p m d", d=d), AX.X, ALU.add))

        def mean_ready(E, at, n, d):
            E.e.tensor_scalar(ms[:, at:at + n], ms[:, at:at + n], 1.0 / d, EPS, ALU.mult, ALU.add).then_inc(ms_ready, 1)

        def turned(E, x, n, f, parts, y, z, z0):
            e = E.e
            d = x.shape[3]
            e.tensor_tensor(y, x, over_heads(CT[:, :, f:f + d], n), ALU.mult)
            for a, w in parts:
                h = w // 2
                for i0, i1 in ((a, a + h), (a + h, a)):
                    i = e.tensor_tensor(z[:, :, :, i0 - z0:i0 - z0 + h], x[:, :, :, i1:i1 + h],
                                        over_heads(ST[:, :, f + i0:f + i0 + h], n), ALU.mult)
            return i

        def lo_block(blk):
            return (x_hi, x_lo)[blk // KX][:, blk % KX, :]

        def qk_stage(E, units, scaled=(), alone=False):
            e = E.e
            for blocks in units:
                pb = bank[7 if alone else 4 + E.qk.n % 4]
                if E.kind == "pe":
                    e.wait_ge(qk_src, E.qks.at())
                    wait(e, qk_lo, E.qk.at(0 if alone else 1 - 4))
                    for b, (blk, src, w) in enumerate(blocks):
                        for tb in range(TB):
                            i = e.transpose(pb[0:w, b * S + tb * P:b * S + (tb + 1) * P], src(tb), ident[:, :])
                    i.then_inc(qk_full, 1)
                if E.kind == "act":
                    e.wait_ge(qk_full, E.qk.at(1))
                    for b, (blk, src, w) in enumerate(blocks):
                        i = nc.scalar.mul(qk_t[0:w, blk, :], pb[0:w, b * S:(b + 1) * S],
                                          HD ** -0.5 if blk in scaled else 1.0)
                    i.then_inc(qk_hi, 1)
                if E.kind == "dve":
                    e.wait_ge(qk_hi, E.qk.at(1))
                    for b, (blk, src, w) in enumerate(blocks):
                        i = e.scalar_tensor_tensor(lo_block(blk)[0:w, :], pb[0:w, b * S:(b + 1) * S],
                                                   HD ** -0.5 if blk in scaled else 1.0, qk_t[0:w, blk, :].bitcast(F32),
                                                   ALU.mult, ALU.subtract)
                    i.then_inc(qk_lo, 1)
                E.qk.n += 1

        def attention(E, maps, aside=None):
            e = E.e
            M = len(maps)
            if E.kind == "pe":
                e.wait_ge(qk_lo, E.qk.at())
                wait(e, acc_act, E.acc.at())
                wait(e, acc_dve, E.acc.at())
            for step in range(M + 2):
                m = step
                if m < M:
                    a = maps[m]
                    sbk = bank[m % 2]
                    g = E.map.at(m)
                    sc2 = slice(2 * (m % 4), 2 * (m % 4) + 2)
                    if E.kind == "pe":
                        wait(e, p_ready, g + 1 - 2)
                        if aside:
                            e.wait_ge(qk_lo, E.qk.at())
                        (qb, q0, q1), (kb, k0, k1) = a["q"], a["k"]
                        for tb in range(TB):
                            t = slice(tb * P, (tb + 1) * P)
                            i = mm3(e, sbk[:, tb * S:(tb + 1) * S], qk_t[q0:q1, qb, t],
                                    lo_block(qb)[q0:q1, t], qk_t[k0:k1, kb, :], lo_block(kb)[k0:k1, :],
                                    True, True)
                        i.then_inc(s_full, 1)
                    if E.kind == "dve":
                        e.wait_ge(s_full, g + 1)
                        if "bias" in a:
                            a["bias_wait"](E)
                            wait(e, p_ready, g + 1 - 2)
                            for tb in range(TB):
                                i = e.tensor_tensor_reduce(SS[:, m % 2, tb, :], sbk[:, tb * S:(tb + 1) * S],
                                                           a["bias"][:, tb, :], 1.0, -3.0e38, ALU.add, ALU.max,
                                                           mx[:, 2 * (m % 4) + tb:2 * (m % 4) + tb + 1])
                            E.link(i)
                            if "sink" in a:
                                E.link(e.tensor_scalar(mx[:, sc2], mx[:, sc2], a["sink"], None, ALU.max))
                        else:
                            E.link(e.tensor_reduce(mx[:, sc2], sbk[:, :].rearrange("p (t n) -> p t n", t=TB),
                                                   AX.X, ALU.max))
                        e.tensor_scalar(negm[:, sc2], mx[:, sc2], -a["scale"], None, ALU.mult).then_inc(mx_done, 1)
                    if E.kind == "act":
                        e.wait_ge(mx_done, g + 1)
                        wait(e, pt_full, g + 1 - 2)
                        if "sink" in a:
                            nc.scalar.activation(esink[:, sc2], negm[:, sc2], ACT.Exp, bias=a["sink"], scale=1.0)
                        for tb in range(TB):
                            src = SS[:, m % 2, tb, :] if "bias" in a else sbk[:, tb * S:(tb + 1) * S]
                            j = 2 * (m % 4) + tb
                            i = nc.scalar.activation(PP[:, m % 2, tb, :], src, ACT.Exp, bias=negm[:, j:j + 1],
                                                     scale=a["scale"], accum_out=psum_[:, j:j + 1])
                        i.then_inc(p_ready, 1)
                m = step - 1
                if 0 <= m < M:
                    g = E.map.at(m)
                    tbk = bank[2 + m % 2]
                    if E.kind == "pe":
                        e.wait_ge(p_ready, g + 1)
                        wait(e, (pt_act, pt_dve)[m % 2], g // 2)
                        for kb in range(TB):
                            for tb in range(TB):
                                i = e.transpose(tbk[:, kb * S + tb * P:kb * S + (tb + 1) * P],
                                                PP[:, m % 2, tb, kb * P:(kb + 1) * P], ident[:, :])
                        i.then_inc(pt_full, 1)
                    if E.kind == ("act", "dve")[m % 2]:
                        e.wait_ge(pt_full, g + 1)
                        wait(e, o_full, g + 1 - 2)
                        src = tbk[:, :].rearrange("p (k n) -> p k n", k=TB)
                        if E.kind == "act":
                            nc.scalar.copy(PT[:, m % 2, :, :], src).then_inc(pt_act, 1)
                        else:
                            e.tensor_copy(PT[:, m % 2, :, :], src).then_inc(pt_dve, 1)
                m = step - 2
                if 0 <= m < M:
                    a = maps[m]
                    g = E.map.at(m)
                    w = a["width"]
                    ob = bank[4 + m % 3]
                    sc2 = slice(2 * (m % 4), 2 * (m % 4) + 2)
                    if E.kind == "pe":
                        e.wait_ge((pt_act, pt_dve)[m % 2], g // 2 + 1)
                        wait(e, o_done, g + 1 - 3)
                        for tb in range(TB):
                            for kb in range(TB):
                                i = e.matmul(ob[:, tb * w:(tb + 1) * w], PT[:, m % 2, kb, tb * P:(tb + 1) * P],
                                             a["v"](kb), start=kb == 0, stop=kb == TB - 1)
                        i.then_inc(o_full, 1)
                    if E.kind == "dve":
                        if "sink" in a:
                            E.link(e.tensor_tensor(psum_[:, sc2], psum_[:, sc2], esink[:, sc2], ALU.add))
                        E.link(e.reciprocal(rsum[:, sc2], psum_[:, sc2]))
                        if a.get("minus"):
                            E.link(e.tensor_scalar(rsum[:, sc2], rsum[:, sc2], nlam[:, 0:1], None, ALU.mult))
                        e.wait_ge(o_full, g + 1)
                        src = ob[:, 0:TB * w].rearrange("p (t n) -> p t n", t=TB)
                        r = rsum[:, sc2].unsqueeze(2).to_broadcast([P, TB, w])
                        if a.get("minus"):
                            tt = t3[:, 0:TB * w].rearrange("p (t n) -> p t n", t=TB)
                            E.link(e.tensor_tensor(tt, src, r, ALU.mult))
                            i = e.tensor_tensor(a["out"], a["out"], tt, ALU.add)
                        else:
                            i = e.tensor_tensor(a["out"], src, r, ALU.mult)
                        i.then_inc(o_done, 1)
                if aside:
                    aside(step)
            E.map.n += M

        def add_to_x(E, alpha, banks):
            e = E.e
            if E.kind == "dve":
                for c in range(2):
                    for tb in range(TB):
                        x = X[:, tb, c * 512:(c + 1) * 512]
                        i = e.scalar_tensor_tensor(x, x, alpha, banks[2 * tb + c][:, :], ALU.mult, ALU.add)
                    i.then_inc(tp_src, 1)

        def drain_dve(E):
            if E.kind == "dve":
                E.link(E.e.engine_nop())

        def copy_act(dst):
            return lambda b: nc.scalar.copy(dst, b)

        def first_layer(E, l):
            e = E.e
            if E.kind == "dve":
                e.wait_ge(tab_in, (l + 1) * 48)
                for ta, g in ((CT, rowv[:, R_G:R_G + ROPEW]), (ST, rowv[:, R_GS:R_GS + ROPEW])):
                    e.tensor_tensor(ta, ta, g.unsqueeze(1).to_broadcast([P, TB, ROPEW]), ALU.mult)
                for j in range(2):
                    a = R_LAM + 2 * j * DQ
                    i = e.tensor_tensor_reduce(t1[:, 0:DQ], rowv[:, a:a + DQ], rowv[:, a + DQ:a + 2 * DQ], 1.0, 0.0,
                                               ALU.mult, ALU.add, lamv[:, j:j + 1])
                    E.link(i)
                e.engine_nop().then_inc(lam_sum, 1)
            if E.kind == "act":
                e.wait_ge(lam_sum, l + 1)
                nc.scalar.activation(lame[:, :], lamv[:, :], ACT.Exp).then_inc(lam_exp, 1)
            lambda_init = 0.8 - 0.6 * math.exp(-0.3 * l)
            if E.kind == "dve":
                e.wait_ge(lam_exp, l + 1)
                E.link(e.tensor_tensor(nlam[:, :], lame[:, 1:2], lame[:, 0:1], ALU.subtract))
                E.link(e.tensor_scalar(nlam[:, :], nlam[:, :], -lambda_init, None, ALU.add))
            if E.kind == "dve" and l == 0:
                e.engine_nop().then_inc(tp_src, 2)
            norm_transposes(E, colg[:, l, CG_ATTN:CG_ATTN + KD], 0)
            nd, ng = 2 * DH, GH + GKV
            at_q, at_k, at_g = 0, TB * nd, 2 * TB * nd
            at_l = at_g + TB * ng

            def columns(c, w):
                return H[:, :, c:c + w]

            def beside(chunk, hx):
                if hx == 0 and E.kind == "dve" and chunk > 1:
                    e.wait_ge(acc_act, E.acc.at())
                    drain_dve(E)
                if chunk == 2 and hx == 0:
                    if E.kind == "dve":
                        e.engine_nop().then_inc(tp_src, 1)
                        for j, (c, w) in enumerate(((C_CQ, MQR), (C_CKV, MKVR))):
                            for tb in range(TB):
                                m = at_l + 2 * j + tb
                                E.link(e.tensor_tensor_reduce(t1[:, 0:w], H[:, tb, c:c + w], H[:, tb, c:c + w],
                                                              1.0 / w, EPS, ALU.mult, ALU.add, ms[:, m:m + 1]))
                        e.engine_nop().then_inc(ms_ready, 1)
                    rsqrt(E, at_l, 4)
                if chunk >= 3:
                    c, f, at = ((C_DQ, F_DQ, at_q), (C_DK, F_DK, at_k), (C_GQ, F_GQ, at_g))[chunk - 3]
                    x = columns(c, 8 * 64).rearrange("p t (h d) -> p t h d", h=8)
                    y, z = heads_view(t1, 8, 64), heads_view(t2, 8, 64)
                    if hx == 0:
                        if E.kind == "dve":
                            head_squares(E, x, 8, 64, at, t1)
                            mean_ready(E, at, TB * 8, 64)
                        rsqrt(E, at, TB * 8)
                    if hx == 1 and E.kind == "dve":
                        if chunk < 5:
                            E.link(turned(E, x, 8, f, [(0, DQ)], y, z, 0))
                        else:
                            for h0, h1, g in ((0, GH, F_GQ), (GH, GH + GKV, F_GK)):
                                i = turned(E, x[:, :, h0:h1], h1 - h0, g, [(0, GD // 2), (GD // 2, GD // 2)],
                                           y[:, :, h0:h1], z[:, :, h0:h1], 0)
                            E.link(i)
                        E.link(e.tensor_tensor(t1, t1, t2, ALU.add))
                    if hx == 2 and E.kind == "dve":
                        need_rs(E)
                        i = e.tensor_tensor(x, y, scales(at, 8, 64), ALU.mult)
                        if chunk == 5:
                            i.then_inc(qk_src, 1)
                        else:
                            E.link(i)

            for j, (c, w) in enumerate(chunks_in1()):
                def scale_act(b, c=c, w=w):
                    if c == 0:
                        need_scale(E)
                    return nc.scalar.mul(H[:, 0, c:c + w], b[:, 0:w], rsx[:, 0:1])

                def scale_dve(b, c=c, w=w):
                    if c == 0:
                        need_scale(E)
                    return e.tensor_scalar(H[:, 1, c:c + w], b[:, 0:w], rsx[:, 1:2], None, ALU.mult)
                gemm_cols(E, w, scale_act, scale_dve, fresh=c == 0, aside=lambda hx, j=j: beside(j, hx))
            E.qks.n += 1
            nq, nk = MQR // P, MKVR // P
            tp_stage(E, H[:, :, C_CQ:C_CQ + MQR + MKVR], nq + nk, 0, colg[:, l, CG_Q:CG_Q + nq + nk], t_bank=0)
            for kn, kk, w, dst, b0 in ((nq, 0, MH * MQK // 2, QA, 4), (nk, nq, MH * (MNOPE + MV) // 2, KV, 0)):
                if kk == 0:
                    if E.kind == "act":
                        need_rs(E)
                    if E.kind == "pe":
                        wait(e, acc_act, E.acc.at())
                        wait(e, acc_dve, E.acc.at())
                j = at_l + (2 if kk else 0)
                for hx in range(kn):
                    need(E, kk + hx)
                    if kk and kk % 2 and hx == 0 and E.kind == "pe":
                        e.wait_ge(tp_lo, E.tp.at())

                    def use(wh, wl, hx=hx, w=w, kn=kn, kk=kk, b0=b0):
                        for c in range(2):
                            for tb in range(TB):
                                t = slice(tb * P, (tb + 1) * P)
                                i = mm3(e, bank[b0 + 2 * c + tb][:, 0:w], x_hi[:, kk + hx, t], x_lo[:, kk + hx, t],
                                        wh[:, c * w:(c + 1) * w], wl[:, c * w:(c + 1) * w], hx == 0, hx == kn - 1)
                        return i
                    E.half_step(use)
                E.acc.n += 1
                if E.kind in ("act", "dve"):
                    e.wait_ge(w_used, E.st.done(-1))
                for c in range(2):
                    if E.kind == "act":
                        i = nc.scalar.mul(dst[:, 0, c * w:(c + 1) * w], bank[b0 + 2 * c][:, 0:w], rs[:, j:j + 1])
                    if E.kind == "dve":
                        i = e.tensor_scalar(dst[:, 1, c * w:(c + 1) * w], bank[b0 + 2 * c + 1][:, 0:w], rs[:, j + 1:j + 2],
                                            None, ALU.mult)
                if E.kind == "act":
                    i.then_inc(acc_act, 1)
                if E.kind == "dve":
                    i.then_inc(acc_dve, 1)
            if E.kind == "pe":
                e.wait_ge(acc_act, E.acc.at(-1))
                e.wait_ge(acc_dve, E.acc.at(-1))
            def blk(src, c, w):
                return lambda tb: src[:, tb, c:c + w]
            blocks = [(j, blk(H, C_DQ + j * P, P), P) for j in range(2 * DH)]
            nb = 2 * DH
            gg = GH // GKV
            blocks += [(nb + j, blk(H, C_GQ + j * P, P), P) for j in range(gg + 1)]
            nb += (GH + GKV) // 2
            qk_stage(E, [blocks[j:j + 2] for j in range(0, len(blocks), 2)])
            def place(n):
                return nb + n if nb + n < N_QK else nb + n - N_QK

            latent = [[(place(2 * j), blk(QA, j * MQK, MQK), MQK), (place(2 * j + 1), blk(KA, j * MQK, MQK), MQK)]
                      for j in range(MH)]
            made = 7
            assert made + (N_QK - N_QK1) // 2 >= 2 * DH

            def latent_heads(step):
                if E.kind == "dve":
                    y = sc_mla[:, 0:TB * MH * MQK]
                    z = sc_mla[:, TB * MH * MQK:TB * MH * (MQK + MROPE)]
                    q4 = QA.rearrange("p t (h d) -> p t h d", h=MH)
                    k4 = KA.rearrange("p t (h d) -> p t h d", h=MH)
                    kn = KV.rearrange("p t (h d) -> p t h d", h=MH)[:, :, :, 0:MNOPE]
                    kr = columns(C_KR, MROPE).unsqueeze(2)
                    nq_, yk = TB * MH, y[:, 0:TB * MH * MNOPE]
                    yq, zq = heads_view(y, MH, MQK), heads_view(z, MH, MROPE)
                    if step == 0:
                        e.wait_ge(acc_act, E.acc.at())
                        drain_dve(E)
                        head_squares(E, q4, MH, MQK, 0, y)
                    if step == 1:
                        head_squares(E, kn, MH, MNOPE, nq_, yk)
                        for tb in range(TB):
                            E.link(e.tensor_tensor_reduce(z[:, 0:MROPE], kr[:, tb, 0], kr[:, tb, 0], 1.0, 0.0,
                                                          ALU.mult, ALU.add, ssk[:, tb:tb + 1]))
                        m = ms[:, nq_:2 * nq_].rearrange("p (t h) -> p t h", t=TB)
                        E.link(e.tensor_tensor(m, m, ssk.unsqueeze(2).to_broadcast([P, TB, MH]), ALU.add))
                        mean_ready(E, 0, 2 * nq_, MQK)
                    if step == 2:
                        E.link(turned(E, q4, MH, F_MQ, [(MNOPE, MROPE)], yq, zq, MNOPE))
                        E.link(e.tensor_tensor(yq[:, :, :, MNOPE:MQK], yq[:, :, :, MNOPE:MQK], zq, ALU.add))
                    if step == 3:
                        need_rs(E)
                        E.link(e.tensor_tensor(q4, yq, scales(0, MH, MQK), ALU.mult))
                    if step == 4:
                        y1 = kr1.rearrange("p (t h d) -> p t h d", t=TB, h=1)
                        z1 = kr2.rearrange("p (t h d) -> p t h d", t=TB, h=1)
                        turned(E, kr, 1, F_MK + MNOPE, [(0, MROPE)], y1, z1, 0)
                        E.link(e.tensor_tensor(heads_view(yk, MH, MNOPE), kn,
                                               over_heads(CT[:, :, F_MK:F_MK + MNOPE], MH), ALU.mult))
                        E.link(e.tensor_tensor(kr1, kr1, kr2, ALU.add))
                    if step == 5:
                        e.tensor_tensor(k4[:, :, :, 0:MNOPE], heads_view(yk, MH, MNOPE), scales(nq_, MH, MNOPE), ALU.mult)
                        kb = kr1.rearrange("p (t h d) -> p t h d", t=TB, h=1)
                        for tb in range(TB):
                            r = rs[:, nq_ + tb * MH:nq_ + (tb + 1) * MH].unsqueeze(2).to_broadcast([P, MH, MROPE])
                            i = e.tensor_tensor(k4[:, tb, :, MNOPE:MQK], kb[:, tb].to_broadcast([P, MH, MROPE]), r,
                                                ALU.mult)
                        i.then_inc(qk_src, 1)
                        drain_dve(E)
                if step == 1:
                    rsqrt(E, 0, 2 * TB * MH)
                if step == 5:
                    E.qks.n += 1
                if made <= step < made + MH:
                    qk_stage(E, [latent[step - made]], alone=True)
            maps = []
            for h in range(DH):
                for c in range(2):
                    o = MH * MV + h * DV
                    maps.append(dict(q=(h, c * 64, c * 64 + 64), k=(DH + h, c * 64, c * 64 + 64),
                                     scale=DQ ** -0.5, width=DV, minus=c == 1,
                                     v=lambda kb, h=h: H[:, kb, C_DV + h * DV:C_DV + (h + 1) * DV],
                                     out=O[:, :, o:o + DV]))
            for h in range(GH):
                kv = h // gg
                maps.append(dict(q=(2 * DH + h % gg, kv * 64, kv * 64 + 64), k=(2 * DH + gg, kv * 64, kv * 64 + 64),
                                 scale=GD ** -0.5, width=GD,
                                 v=lambda kb, kv=kv: H[:, kb, C_GV + kv * GD:C_GV + (kv + 1) * GD],
                                 out=O[:, :, MH * MV + DH * DV + h * GD:MH * MV + DH * DV + (h + 1) * GD]))
            for h in range(MH):
                maps.append(dict(q=(place(2 * h), 0, MQK), k=(place(2 * h + 1), 0, MQK), scale=MQK ** -0.5, width=MV,
                                 v=lambda kb, h=h: KV[:, kb, h * P + MNOPE:(h + 1) * P],
                                 out=O[:, :, h * MV:(h + 1) * MV]))
            attention(E, maps, latent_heads)
            if E.kind == "dve":
                drain_dve(E)
                for tb in range(TB):
                    x = O[:, tb, MH * MV:MH * MV + DH * DV]
                    y = t1[:, 0:DH * DV]
                    E.link(e.tensor_tensor(y, x, x, ALU.mult))
                    E.link(e.tensor_reduce(ms[:, tb * DH:(tb + 1) * DH], y.rearrange("p (h d) -> p h d", h=DH),
                                           AX.X, ALU.add))
                e.tensor_scalar(ms[:, 0:2 * DH], ms[:, 0:2 * DH], 1.0 / DV, EPS, ALU.mult, ALU.add).then_inc(
                    ms_ready, 1)
            rsqrt(E, 0, 2 * DH)
            if E.kind == "dve":
                need_rs(E)
                for tb in range(TB):
                    x = O[:, tb, MH * MV:MH * MV + DH * DV].rearrange("p (h d) -> p h d", h=DH)
                    E.link(e.tensor_tensor(x, x, rs[:, tb * DH:(tb + 1) * DH].unsqueeze(2).to_broadcast(
                        [P, DH, DV]), ALU.mult))
                    i = e.scalar_tensor_tensor(x, x, 1.0 - lambda_init, rowv[:, R_OG:R_OG + DV].unsqueeze(
                        1).to_broadcast([P, DH, DV]), ALU.mult, ALU.mult)
                i.then_inc(tp_src, 1)
            tp_stage(E, O, MIX // P, 0)
            gemm_rows(E, MIX // P, 0)
            if E.kind == "dve":
                e.wait_ge(w_used, E.st.done(-1))
            add_to_x(E, 1.0, bank[0:4])
            norm_transposes(E, colg[:, l, CG_FFN:CG_FFN + KD], 4)
            if l + 1 < LAYERS:
                pool_tables(E, l + 1)
            else:
                pool_ln(E, 0)
            ffn(E, FF1 // FC, TB, scaled=True)
            if E.kind == "dve":
                e.wait_ge(w_used, E.st.done(-1))
            if l + 1 < LAYERS:
                add_to_x(E, 1.0, bank[4:8])
            else:
                residual_norm(E, 1.0, bank[4:8])

        def ffn(E, nc_, tbs, t0=0, hook=None, scaled=False):
            e = E.e
            T = tbs * P
            if E.kind == "pool":
                return

            def gu_half(hx, fresh=False):
                def use(wh, wl):
                    for j in range(2):
                        k = 2 * hx + j
                        w = slice(j * 512, (j + 1) * 512)
                        for tb in range(tbs):
                            t = slice(t0 + tb * P, t0 + (tb + 1) * P)
                            i = mm3(e, bank[tb][:, :], x_hi[:, k, t], x_lo[:, k, t], wh[:, w], wl[:, w],
                                    k == 0, k == KD - 1)
                    return i
                if E.kind == "pe" and hx == 0:
                    wait(e, h_ready, E.ff.at())
                if fresh:
                    need(E, 2 * hx)
                E.half_step(use)

            def turn(step=None):
                n = E.ff.at()
                if tbs == 1:
                    tr = [bank[2][:, f * T:(f + 1) * T] for f in range(2)]
                else:
                    tr = [bank[2 + f][:, 0:T] for f in range(2)]
                more = hook if hook is not None and step is not None else lambda step: None
                if E.kind == "pe":
                    e.wait_ge(h_ready, n)
                    for f in range(2):
                        for tb in range(tbs):
                            i = e.transpose(tr[f][:, tb * P:(tb + 1) * P], HH[:, tb, f * P:(f + 1) * P], ident[:, :])
                    (more(step) or i).then_inc(ht_full, 1)
                if E.kind == "act":
                    e.wait_ge(ht_full, n)
                    for f in range(2):
                        i = nc.scalar.copy(hT_hi[:, f, 0:T], tr[f])
                    (more(step) or i).then_inc(ht_hi, 1)
                if E.kind == "dve":
                    e.wait_ge(ht_hi, n)
                    for f in range(2):
                        i = e.tensor_tensor(hT_lo[:, f, 0:T], tr[f], hT_hi[:, f, 0:T].bitcast(F32), ALU.subtract)
                    (more(step) or i).then_inc(ht_lo, 1)

            def act_mul():
                n = E.ff.at(1)
                if E.kind == "act":
                    e.wait_ge(w_used, E.st.done(-1))
                    for tb in range(tbs):
                        i = nc.scalar.activation(SIL[:, tb, :], bank[tb][:, 0:FC], ACT.Silu,
                                                 scale=rsx[:, tb:tb + 1] if scaled else 1.0)
                    i.then_inc(sil_done, 1)
                if E.kind == "dve":
                    e.wait_ge(sil_done, n)
                    for tb in range(tbs):
                        up = bank[tb][:, FC:2 * FC]
                        if scaled:
                            i = e.scalar_tensor_tensor(HH[:, tb, :], up, rsx[:, tb:tb + 1], SIL[:, tb, :],
                                                       ALU.mult, ALU.mult)
                        else:
                            i = e.tensor_tensor(HH[:, tb, :], SIL[:, tb, :], up, ALU.mult)
                    i.then_inc(h_ready, 1)

            def down(hx, first, last):
                def use(wh, wl):
                    for tb in range(tbs):
                        t = slice(tb * P, (tb + 1) * P)
                        for c in range(2):
                            w = slice(c * 512, (c + 1) * 512)
                            i = mm3(e, bank[4 + 2 * tb + c][:, :], hT_hi[:, hx, t], hT_lo[:, hx, t],
                                    wh[:, w], wl[:, w], first and hx == 0, last and hx == 1)
                    return i
                if E.kind == "pe" and hx == 0:
                    e.wait_ge(ht_lo, E.ff.at())
                E.half_step(use)

            def chunk(first=False, step=None):
                gu_half(0)
                gu_half(1)
                turn(step)
                gu_half(2)
                gu_half(3)
                act_mul()
                down(0, first, False)
                down(1, first, False)
                E.ff.n += 1

            for hx in range(4):
                gu_half(hx, fresh=hook is None)
            if scaled and E.kind in ("act", "dve"):
                need_scale(E)
            act_mul()
            E.ff.n += 1
            if hook is not None:
                hook(0)
            peeled = 2 if hook is None else 8
            for c in range(1, peeled + 1):
                chunk(first=c == 1, step=c)
            loops = (nc_ - 1 - peeled) // 2
            s0, p0 = E.st.s, E.st.periods
            with e.Fori(0, loops) as i:
                E.st.periods = p0 + i
                E.ff.enter(i, 2)
                chunk()
                chunk()
                E.ff.leave(loops)
            E.st.s, E.st.periods = s0 + loops * PERIOD, p0
            if (nc_ - 1) % 2:
                chunk()
            turn()
            down(0, False, True)
            down(1, False, True)

        def residual_norm(E, alpha, banks):
            e = E.e
            if E.kind == "dve":
                for tb in range(TB):
                    for c in range(2):
                        x = X[:, tb, c * 512:(c + 1) * 512]
                        i = e.scalar_tensor_tensor(x, x, alpha, banks[2 * tb + c][:, :], ALU.mult, ALU.add,
                                                   accum_out=sx[:, 2 * tb + c:2 * tb + c + 1])
                    E.link(i)
                    E.link(e.tensor_tensor(negmu[:, tb:tb + 1], sx[:, 2 * tb:2 * tb + 1], sx[:, 2 * tb + 1:2 * tb + 2],
                                           ALU.add))
                    e.tensor_scalar(negmu[:, tb:tb + 1], negmu[:, tb:tb + 1], -1.0 / D, None, ALU.mult).then_inc(
                        mu_ready, 1)
            square_sums(E, negmu)
            row_scale(E, LN_EPS)
            if E.kind == "dve":
                e.wait_ge(lnb_in, E.ln.at(1) * 16)
                e.wait_ge(mu_ready, TB * E.ln.at(1))
                for tb in range(TB):
                    i = e.scalar_tensor_tensor(XS[:, tb, :], X[:, tb, :], negmu[:, tb:tb + 1], GB[:, 0:D],
                                               ALU.add, ALU.mult)
                E.link(i)
                need_scale(E)
                for c in range(2):
                    w = slice(c * 512, (c + 1) * 512)
                    for tb in range(TB):
                        i = e.scalar_tensor_tensor(X[:, tb, w], XS[:, tb, w], rsx[:, tb:tb + 1],
                                                   GB[:, D + c * 512:D + (c + 1) * 512], ALU.mult, ALU.add)
                    i.then_inc(tp_src, 1)
            E.ln.n += 1

        def second_mixer(E, l):
            e = E.e
            tp_stage(E, X, KD, 0, parts=2, t_bank=0)
            n_qkv = len([c for c in chunks_in2() if c[0] < W_QKV2])
            for j, (c, w) in enumerate(chunks_in2()):
                if j < n_qkv:
                    gemm_cols(E, w, lambda b, c=c, w=w: nc.scalar.copy(H2[:, 0, c:c + w], b[:, 0:w]),
                              lambda b, c=c, w=w: e.tensor_copy(H2[:, 1, c:c + w], b[:, 0:w]), fresh=c == 0)
                else:
                    g = c - W_QKV2
                    bias = (BG if g < D else BG2)[:, g % D:g % D + 512]

                    def both(b, g=g, bias=bias):
                        b0, b1 = bank[4 + 2 * (E.acc.n % 2)], bank[5 + 2 * (E.acc.n % 2)]
                        e.wait_ge(bg_in, (l + 1) * 64)
                        e.tensor_tensor(G2[:, 0, g:g + 512], b0[:, :], bias, ALU.add)
                        return e.tensor_tensor(G2[:, 1, g:g + 512], b1[:, :], bias, ALU.add)

                    def gates(b, g=g):
                        e.wait_ge(acc_dve, E.acc.at(1))
                        return nc.scalar.activation(G2[:, :, g:g + 512], G2[:, :, g:g + 512], ACT.Sigmoid)
                    gemm_cols(E, w, gates, both)
            if E.kind == "dve":
                e.wait_ge(acc_act, E.acc.at())
                drain_dve(E)
                n = SH + SKV
                for tb in range(TB):
                    x = H2[:, tb, C_QS:C_VS].rearrange("p (h d) -> p h d", h=n)[:, :, 0:ROT]
                    c = rotc[:, tb * ROT:(tb + 1) * ROT].unsqueeze(1).to_broadcast([P, n, ROT])
                    y = t1[:, 0:n * ROT].rearrange("p (h d) -> p h d", h=n)
                    z = t2[:, 0:n * ROT].rearrange("p (h d) -> p h d", h=n)
                    e.tensor_tensor(y, x, c, ALU.mult)
                    h = ROT // 2
                    for i0, i1 in ((0, h), (h, 0)):
                        i = e.tensor_tensor(z[:, :, i0:i0 + h], x[:, :, i1:i1 + h],
                                            rots[:, tb * ROT + i0:tb * ROT + i0 + h].unsqueeze(1).to_broadcast(
                                                [P, n, h]), ALU.mult)
                    E.link(i)
                    E.link(e.tensor_tensor(x, y, z, ALU.add))
                e.engine_nop().then_inc(qk_src, 1)
            E.qks.n += 1

            def blk(c):
                return lambda tb: H2[:, tb, c:c + P]
            blocks = [(j, blk(j * P), P) for j in range(NH)]
            sg = SH // SKV
            blocks += [(NH + j, blk(C_QS + j * P), P) for j in range(sg + 1)]
            scaled = set(range(NH // 2)) | {NH + j for j in range(SH // 2)}
            qk_stage(E, [blocks[j:j + 2] for j in range(0, len(blocks), 2)], scaled)
            maps = []
            for h in range(NH):
                p0 = h % 2 * 64

                def bias_wait(E, h=h):
                    E.e.wait_ge(bt_in[h % (NBT - 1)], 16 * (l * (NH // (NBT - 1)) + h // (NBT - 1) + 1))
                maps.append(dict(q=(h // 2, p0, p0 + 64), k=(NH // 2 + h // 2, p0, p0 + 64), scale=1.0,
                                 width=HD, bias=BT[:, h % (NBT - 1)], bias_wait=bias_wait,
                                 v=lambda kb, h=h: H2[:, kb, 2 * W_NA + h * HD:2 * W_NA + (h + 1) * HD],
                                 out=O[:, :, h * HD:(h + 1) * HD]))
            for h in range(SH):
                kv = h // sg
                maps.append(dict(q=(NH + h % sg, kv * 64, kv * 64 + 64), k=(NH + sg, kv * 64, kv * 64 + 64),
                                 scale=1.0, width=HD, bias=BT[:, NBT - 1], bias_wait=lambda E: None,
                                 sink=sinkb[:, h:h + 1],
                                 v=lambda kb, kv=kv: H2[:, kb, C_VS + kv * HD:C_VS + (kv + 1) * HD],
                                 out=O[:, :, W_NA + h * HD:W_NA + (h + 1) * HD]))
            if E.kind == "dve":
                e.wait_ge(bg_in, (l + 1) * 64)
            attention(E, maps)
            if E.kind == "dve":
                e.engine_nop().then_inc(tp_src, 1)
            tp_stage(E, O[:, :, 0:D], KD, 0)
            gemm_rows(E, W_NA // P, 0)
            scalar_rows(E, lambda tb, c, b: e.tensor_tensor(
                YG[:, tb, c * 512:(c + 1) * 512], b, G2[:, tb, c * 512:(c + 1) * 512], ALU.mult))
            if E.kind == "dve":
                drain_dve(E)
            if E.kind == "pe":
                e.wait_ge(tp_lo, E.tp.at())
            gemm_rows(E, W_NA // P, W_NA // P, b0=4)

            def add_sw(tb, c, b):
                g = G2[:, tb, D + c * 512:D + (c + 1) * 512]
                E.link(e.tensor_tensor(t1[:, 0:512], b, g, ALU.mult))
                E.link(e.tensor_tensor(YG[:, tb, c * 512:(c + 1) * 512], YG[:, tb, c * 512:(c + 1) * 512],
                                       t1[:, 0:512], ALU.add))

            scalar_rows(E, add_sw, b0=4)
            if E.kind == "dve":
                e.engine_nop().then_inc(tp_src, 1)
            tp_stage(E, YG, KD, 0)
            gemm_rows(E, KD, 0)
            if E.kind == "dve":
                e.wait_ge(w_used, E.st.done(-1))
            residual_norm(E, ALPHA, bank[0:4])

        def moe(E):
            e = E.e
            if E.kind == "pool":
                return
            tp_stage(E, X, KD, 0, parts=2)
            if E.kind == "act":
                nc.scalar.copy(rw_hi[:, :, :], router[:, :, :]).then_inc(
                    rw_split, 1)
            if E.kind == "dve":
                e.wait_ge(rw_split, 1)
                e.tensor_tensor(rw_lo[:, :, :], router[:, :, :],
                                rw_hi[:, :, :].bitcast(F32), ALU.subtract).then_inc(rw_split, 1)
            if E.kind == "pe":
                e.wait_ge(rw_split, 2)
                e.wait_ge(tp_lo, E.tp.at())
                for tb in range(TB):
                    t = slice(tb * P, (tb + 1) * P)
                    n = 0
                    for k in range(KD):
                        for a in (x_hi, x_lo):
                            for b in (rw_hi, rw_lo):
                                i = e.matmul(bank[tb][:, 0:NE], a[:, k, t], b[:, k, :], start=n == 0,
                                             stop=n == 4 * KD - 1)
                                n += 1
                i.then_inc(lg_full, 1)
            if E.kind == "dve":
                e.wait_ge(lg_full, 1)
                for tb in range(TB):
                    i = e.tensor_copy(lg[:, tb * 8:(tb + 1) * 8], bank[tb][:, 0:NE])
                E.link(i)
                for tb in range(TB):
                    i = e.max(m8[:, tb * 8:(tb + 1) * 8], lg[:, tb * 8:(tb + 1) * 8])
                E.link(i)
                for tb in range(TB):
                    i = e.max_index(idx[:, tb, :], m8[:, tb * 8:(tb + 1) * 8], lg[:, tb * 8:(tb + 1) * 8])
                E.link(i)
                E.link(e.tensor_copy(ixf.rearrange("p (t n) -> p t n", t=TB), idx[:, :, :]))
                m3 = m8.rearrange("p (t n) -> p t n", t=TB)
                x3 = ixf.rearrange("p (t n) -> p t n", t=TB)
                io = iota8.unsqueeze(1).to_broadcast([P, TB, 8])
                v3 = lambda a: a.rearrange("p (t n) -> p t n", t=TB)
                e.tensor_tensor(v3(oh0), io, x3[:, :, 0:1].to_broadcast([P, TB, 8]), ALU.is_equal)
                e.tensor_tensor(v3(oh1), io, x3[:, :, 1:2].to_broadcast([P, TB, 8]), ALU.is_equal)
                e.tensor_tensor(dv.unsqueeze(2), m3[:, :, 1:2], m3[:, :, 0:1], ALU.subtract).then_inc(top_done, 1)
                e.wait_ge(exp_done, 1)
                E.link(e.tensor_scalar(w1, ev, 1.0, None, ALU.add))
                E.link(e.reciprocal(w0, w1))
                E.link(e.tensor_tensor(w1, w0, ev, ALU.mult))
                e.memset(CW, 0.0)
                E.link(e.memset(POS, -1.0))
                cw3, ps3 = [a.rearrange("p (t n) -> p t n", t=TB)[:, :, 0:NE] for a in (CW, POS)]
                e.tensor_tensor(cw3, v3(oh0), w0.unsqueeze(2).to_broadcast([P, TB, 8]), ALU.mult)
                E.link(e.tensor_tensor(v3(tmp8), v3(oh1), w1.unsqueeze(2).to_broadcast([P, TB, 8]), ALU.mult))
                E.link(e.tensor_tensor(cw3, cw3, v3(tmp8), ALU.add))
                e.tensor_tensor(MSK, oh0, oh1, ALU.add).then_inc(route, 1)
            if E.kind == "act":
                e.wait_ge(top_done, 1)
                nc.scalar.activation(ev, dv, ACT.Exp).then_inc(exp_done, 1)
            if E.kind == "pe":
                e.wait_ge(route_in, 32)
                e.wait_ge(route, 1)
                e.matmul(bank[2][:, 0:8], tri[:, :], MSK[:, 0:8], start=True, stop=True)
                e.matmul(bank[2][:, 8:16], ones[:, :], MSK[:, 0:8], start=True, stop=False)
                e.matmul(bank[2][:, 8:16], tri[:, :], MSK[:, 8:16], start=False, stop=True)
                e.matmul(bank[2][:, 16:24], ones[:, :], MSK[:, 0:8], start=True, stop=False)
                e.matmul(bank[2][:, 16:24], ones[:, :], MSK[:, 8:16], start=False, stop=True).then_inc(pos_full, 1)
            if E.kind == "dve":
                e.wait_ge(pos_full, 1)
                E.link(e.tensor_scalar(ps3, bank[2][:, 0:16].rearrange("p (t n) -> p t n", t=TB), 1.0, None, ALU.add))
                E.link(e.tensor_tensor(ps3, ps3, v3(MSK), ALU.mult))
                E.link(e.tensor_scalar(ps3, ps3, -1.0, None, ALU.add))
                E.link(e.tensor_reduce(cntm[:, 0:1], bank[2][:, 16:24], AX.X, ALU.max))
                E.link(e.tensor_scalar(cntm[:, 1:2], cntm[:, 0:1], float(P) + 0.5, None, ALU.is_gt))
                e.tensor_copy(flag[:, 0:1], cntm[:, 1:2]).then_inc(plan_done, 1)
            experts(E, 0)
            if E.kind in ("pe", "act", "dve"):
                e.wait_ge(plan_done, 1)
                over = e.value_load(flag[0:1, 0:1], min_val=0, max_val=1)
                with e.If(over > 0):
                    experts(E, 1)
                    if E.kind == "pe":
                        e.wait_ge(ye_ready, 2 * NE)
            if E.kind == "pe":
                e.wait_ge(ye_ready, NE)
                scatter(E, 1, last=True)

        def select(E, e_col, part):
            e = E.e
            if E.kind == "dve":
                for tb in range(TB):
                    pos = POS[:, tb * XW:(tb + 1) * XW][:, e_col]
                    cw = CW[:, tb * XW:(tb + 1) * XW][:, e_col]
                    io = iota[:, part * P:(part + 1) * P]
                    e.tensor_scalar(SE[:, tb, :], io, pos, None, ALU.is_equal)
                    i = e.tensor_scalar(SW[:, tb, :], io, pos, cw, ALU.is_equal, ALU.mult)
                i.then_inc(se_ready, 1)

        def gather_piece(E, p, buf):
            e = E.e
            out = bank[2][:, 2 * P:4 * P]
            o3 = out.rearrange("p (k n) -> p k n", n=P)
            t = slice(buf * P, (buf + 1) * P)
            if E.kind == "pe":
                for j in range(2):
                    o = out[:, j * P:(j + 1) * P]
                    if p < KD // 2:
                        k = 2 * p + j
                        for tb in range(TB):
                            i = e.matmul(o, X[:, tb, k * P:(k + 1) * P], SE[:, tb, :], start=tb == 0,
                                         stop=tb == TB - 1)
                    else:
                        i = e.transpose(o, SW[:, j, :], ident[:, :])
                return i
            if E.kind == "act":
                if p < KD // 2:
                    return nc.scalar.copy(x_hi[:, 2 * p:2 * p + 2, t], o3)
                return nc.scalar.copy(SWT[:, buf, :], out)
            if E.kind == "dve" and p < KD // 2:
                return e.tensor_tensor(x_lo[:, 2 * p:2 * p + 2, t], o3, x_hi[:, 2 * p:2 * p + 2, t].bitcast(F32),
                                       ALU.subtract)

        def scatter(E, buf, first=False, last=False):
            e = E.e
            for tb in range(TB):
                for c in range(2):
                    i = e.matmul(sum_bank[2 * tb + c][:, :], SWT[:, buf, tb * P:(tb + 1) * P],
                                 YE[:, c * 512:(c + 1) * 512], start=first, stop=last, skip_group_check=True)
            if last:
                i.then_inc(sc_full, 1)

        def experts(E, part):
            e = E.e
            pieces = KD // 2 + 1
            if E.kind == "act" and part == 0:
                for zero in (YE.rearrange("p (b n) -> p b n", n=S), SWT[:, :, :]):
                    i = nc.scalar.mul(zero, iota[:, :].unsqueeze(1).to_broadcast([P, zero.shape[1], S]), 0.0)
                i.then_inc(ye_zero, 1)
            if E.kind == "pe" and part == 0:
                e.wait_ge(ye_zero, 1)
                scatter(E, 1, first=True)
            select(E, slice(0, 1), part)
            for p in range(pieces):
                n = part * pieces + p + 1
                if E.kind == "pe":
                    if p == 0:
                        e.wait_ge(se_ready, part * (NE + 1) + 1)
                    else:
                        e.wait_ge(xe_lo, n - 1)
                    gather_piece(E, p, 0).then_inc(xe_full, 1)
                if E.kind == "act":
                    e.wait_ge(xe_full, n)
                    gather_piece(E, p, 0).then_inc(xe_hi, 1)
                if E.kind == "dve":
                    e.wait_ge(xe_hi, n)
                    i = gather_piece(E, p, 0)
                    (i if i is not None else e.engine_nop()).then_inc(xe_lo, 1)
            if E.kind == "pe":
                e.wait_ge(xe_lo, (part + 1) * pieces)
            s0 = E.st.s
            with e.Fori(0, NE // 2) as x:
                for buf in range(2):
                    E.st.s = MOE_AT + buf * H_EXP
                    E.st.periods = x * (2 * H_EXP // PERIOD) + part * (NE * H_EXP // PERIOD)
                    if buf == 0:
                        E.ff.enter(x, 2 * (FFE // FC))
                    n = x * 2 + (part * NE + buf + 1)
                    nxt = bass.ds(x * 2 + (buf + 1), 1)

                    def hook(step, buf=buf, n=n, nxt=nxt, part=part):
                        if step == 0:
                            select(E, nxt, part)
                            if E.kind == "pe":
                                e.wait_ge(ye_ready, n - 1)
                                scatter(E, 1 - buf)
                                e.wait_ge(se_ready, n + (part + 1))
                        elif 2 <= step < 2 + pieces:
                            return gather_piece(E, step - 2, 1 - buf)
                    ffn(E, FFE // FC, 1, buf * P, hook)
                    if E.kind == "act":
                        e.wait_ge(w_used, E.st.done(-1))
                        for c in range(2):
                            i = nc.scalar.copy(YE[:, c * 512:(c + 1) * 512], bank[4 + c][:, :])
                        i.then_inc(ye_ready, 1)
                E.ff.leave(NE // 2)
            E.st.s = MOE_AT + NE * H_EXP
            E.st.periods = part * (NE * H_EXP // PERIOD)
            if part == 1:
                E.st.s = s0
                E.st.periods = 0

        def program(E):
            e = E.e
            if E.kind == "act":
                e.wait_ge(c_in, N_CONST * 16)
            if E.kind == "dve":
                e.memset(half_c, -0.5).then_inc(half_set, 1)
                e.wait_ge(half_set, 1)
                e.wait_ge(c_in, N_CONST * 16)
                e.wait_ge(x_in, 16)
                E.link(e.memset(ms, 1.0))
            if E.kind == "pe":
                e.wait_ge(c_in, N_CONST * 16)
            if E.kind == "pool":
                e.wait_ge(half_set, 1)
            E.prologue()
            pool_tables(E, 0)
            for l in range(LAYERS):
                first_layer(E, l)
            for l in range(LAYERS):
                pool_ln(E, 1 + 2 * l)
                pool_mixer(E, l)
                second_mixer(E, l)
                pool_ln(E, 2 + 2 * l)
                if l == 0:
                    tp_stage(E, X, KD, 0, parts=2)
                    ffn(E, FF1 // FC, TB)
                    if E.kind == "dve":
                        e.wait_ge(w_used, E.st.done(-1))
                    residual_norm(E, ALPHA, bank[4:8])
                else:
                    moe(E)
                    if E.kind == "dve":
                        e.wait_ge(sc_full, 1)
                    residual_norm(E, ALPHA, sum_bank)

        def pool_tables(E, l):
            if E.kind == "pool":
                e = E.e
                e.dma_start(CT, A["ropec"].rearrange("(t p) n -> p t n", p=P)).then_inc(tab_in, 16)
                e.dma_start(ST, A["ropes"].rearrange("(t p) n -> p t n", p=P)).then_inc(tab_in, 16)
                e.dma_start(rowv, A["rowv"][l:l + 1, :].to_broadcast([P, ROWV])).then_inc(tab_in, 16)

        def pool_ln(E, n):
            if E.kind == "pool":
                e = E.e
                if n:
                    e.wait_ge(tp_src, E.src.at(2))
                if n == 0:
                    e.dma_start(tri, A["tri"]).then_inc(route_in, 16)
                    e.dma_start(ones, A["ones"]).then_inc(route_in, 16)
                e.dma_start(GB, A["lngb"][n:n + 1, :].to_broadcast([P, 2 * D])).then_inc(lnb_in, 16)

        def pool_mixer(E, l):
            if E.kind != "pool":
                return
            e = E.e
            if l:
                e.wait_ge(o_done, LAYERS * N_MAP1 + l * N_MAP2)
                e.wait_ge(h_ready, (LAYERS + l) * (FF1 // FC))
            e.dma_start(BG, A["bgate"][l:l + 1, 0:D].to_broadcast([P, D])).then_inc(bg_in, 16)
            e.dma_start(BG2, A["bgate"][l:l + 1, D:2 * D].to_broadcast([P, D])).then_inc(bg_in, 16)
            e.dma_start(BT[:, NBT - 1], A["band"].rearrange("(t p) n -> p t n", p=P)).then_inc(bg_in, 16)
            e.dma_start(sinkb, A["sink"][l:l + 1, :].to_broadcast([P, SH])).then_inc(bg_in, 16)
            for h in range(NH):
                slot = h % (NBT - 1)
                if h >= NBT - 1:
                    e.wait_ge(mx_done, LAYERS * N_MAP1 + l * N_MAP2 + h - (NBT - 1) + 1)
                e.dma_start(BT[:, slot], A["rpb"][l, h].rearrange("(t p) n -> p t n", p=P)).then_inc(bt_in[slot], 16)

        consts = [(ident[:, :], "ident"), (iota[:, :], "iota"),
                  (router[:, :, :], "router"), (colg[:, :, :], "colg"), (iota8, "iota8"),
                  (rotc.rearrange("p (t n) -> p t n", t=TB), "rotc"), (rots.rearrange("p (t n) -> p t n", t=TB), "rots")]
        N_CONST = len(consts)

        block = ctx.enter_context(nc.Block())

        @block.sync
        def _(sp):
            sp.dma_start(X[:, :, :], A["x"].rearrange("(t p) n -> p t n", p=P)).then_inc(x_in, 16)
            for dst, name in consts:
                src = A[name]
                if name in ("rotc", "rots"):
                    src = src.rearrange("(t p) n -> p t n", p=P)
                sp.dma_start(dst, src).then_inc(c_in, 16)
            stream = A["stream"]

            def load(slot, group, used, free):
                wait(sp, lo_done, free)
                src = stream[group] if isinstance(group, int) else stream[group].rearrange("o p n -> (o p) n")
                sp.dma_start(raw[:, slot, :], src).then_inc(raw_in[slot], 16)
            groups = TOTAL // 2
            for g in range(RAW):
                load(g, g, 0, 0)
            rounds = groups // RAW - 1
            with sp.Fori(0, rounds) as i:
                for s in range(RAW):
                    load(s, bass.ds(i * RAW + (RAW + s), 1), 0, i * PERIOD + (2 * s + 2))
            for g in range(RAW * (rounds + 1), groups):
                load(g % RAW, g, 0, 2 * (g - RAW) + 2)
            first = MOE_AT // 2
            for g in range(groups, groups + LEAD):
                load(g % RAW, g - groups + first, 0, 2 * (g - RAW) + 2)
            sp.wait_ge(plan_done, 1)
            over = sp.value_load(flag[0:1, 0:1], min_val=0, max_val=1)
            with sp.If(over > 0):
                n = groups - first
                rounds2 = (n - LEAD) // RAW
                with sp.Fori(0, rounds2) as i:
                    for s in range(LEAD, LEAD + RAW):
                        load((groups + s) % RAW, bass.ds(i * RAW + (first + s), 1), 0,
                             i * PERIOD + (2 * (groups + s - RAW) + 2))
                for s in range(LEAD + rounds2 * RAW, n + LEAD):
                    load((groups + s) % RAW, first + s % n, 0, 2 * (groups + s - RAW) + 2)
            for c in range(2):
                sp.wait_ge(tp_src, SOURCES - 1 + c)
                w = slice(c * 512, (c + 1) * 512)
                sp.dma_start(A["out"].rearrange("(t p) n -> p t n", p=P)[:, :, w], X[:, :, w]).then_inc(out_done, 16)
            sp.wait_ge(out_done, 32)

        @block.tensor
        def _(pe):
            program(Eng(pe, "pe"))

        @block.scalar
        def _(act):
            program(Eng(act, "act"))

        @block.vector
        def _(dve):
            program(Eng(dve, "dve"))

        @block.gpsimd
        def _(pool):
            program(Eng(pool, "pool"))


def _halves_cols(w, width):
    k = w.shape[0] // P
    n = w.shape[1]
    per = 4 if n == 256 else 2
    stride = HALF // per
    b = np.zeros((k // per, P, per, stride), np.float32)
    b[..., :n] = w.reshape(k // per, per, P, n).transpose(0, 2, 1, 3)
    return b.reshape(k // per, P, HALF)


def _halves_rows(w):
    k, n = w.shape[0] // P, w.shape[1]
    b = np.zeros((k, P, HALF), np.float32)
    b[:, :, :n] = w.reshape(k, P, n)
    return b


def _ffn(wg, wu, wd):
    n = wg.shape[1] // FC

    def gu(c):
        s = slice(c * FC, (c + 1) * FC)
        return _halves_cols(np.concatenate([wg[:, s], wu[:, s]], 1), 512)

    def dn(c):
        return _halves_rows(wd[c * FC:(c + 1) * FC])
    out = [gu(0)]
    for c in range(1, n):
        out += [gu(c), dn(c - 1)]
    return out + [dn(n - 1)]


def _pair(w, c, kv, group):
    w = w.copy()
    n = kv * group * 64
    w[:, c:c + n] = w[:, c:c + n].reshape(-1, kv, group, 64).transpose(0, 2, 1, 3).reshape(-1, n)
    return w


def _swap(g, parts):
    g = g.copy()
    for a, w in parts:
        h = w // 2
        g[..., a:a + h], g[..., a + h:a + w] = g[..., a + h:a + w].copy(), g[..., a:a + h].copy()
    return g


def _cos_sin(pos, dim, theta):
    inv = 1.0 / (theta ** (np.arange(0, dim, 2, dtype=np.float32) / np.float32(dim)))
    ang = pos.astype(np.float32)[:, None] * inv.astype(np.float32)[None, :]
    return np.cos(ang, dtype=np.float32), np.sin(ang, dtype=np.float32)


def _layout(a):
    f = lambda n: np.asarray(a[n])
    out = {"x": f("x").reshape(S, D)}
    parts = []
    for l in range(LAYERS):
        w = f("w_in")[l]
        v = C_GQ
        w = np.concatenate([w[:, :v], w[:, v + DH * DV:], w[:, v:v + DH * DV]], 1)
        w = _pair(w, C_GQ, GKV, GH // GKV)
        parts += [_halves_cols(w[:, c:c + n], n) for c, n in chunks_in1()]
        parts += [_halves_rows(f("mla_w_uq")[l]), _halves_rows(f("mla_w_ukv")[l]), _halves_rows(f("w_o")[l])]
        g = f("w_gate_up")[l]
        parts += _ffn(g[:, :FF1], g[:, FF1:], f("w_down")[l])
    for l in range(LAYERS):
        w = _pair(f("w_in_2")[l], C_QS, SKV, SH // SKV)
        parts += [_halves_cols(w[:, c:c + n], n) for c, n in chunks_in2()]
        parts += [_halves_rows(f(n)[l]) for n in ("w_branch_na_2", "w_branch_sw_2", "w_out_2")]
        if l == 0:
            parts += _ffn(f("ffn_w_gate_2")[0], f("ffn_w_up_2")[0], f("ffn_w_down_2")[0])
        else:
            for x in range(NE):
                parts += _ffn(f("moe_w_gate_2")[0, x], f("moe_w_up_2")[0, x], f("moe_w_down_2")[0, x])
    s = np.concatenate(parts, 0)
    assert s.shape[0] == TOTAL, (s.shape, TOTAL)
    out["stream"] = np.ascontiguousarray(s.reshape(TOTAL // 2, 2, P, HALF).transpose(0, 2, 1, 3)).reshape(
        TOTAL // 2, P, GROUP)
    col = [f(n).reshape(LAYERS, -1, P) for n in ("attn_norm", "ffn_norm", "mla_q_norm", "mla_kv_norm")]
    out["colg"] = np.ascontiguousarray(np.concatenate(col, 1).transpose(2, 0, 1))
    g = [f(n) for n in ("mla_q_gain", "mla_k_gain", "diff_q_gain", "diff_k_gain", "gqa_q_gain", "gqa_k_gain")]
    ax = [(0, GD // 2), (GD // 2, GD // 2)]
    rot = [[(MNOPE, MROPE)]] * 2 + [[(0, DQ)]] * 2 + [ax] * 2
    out["rowv"] = np.concatenate(g + [_swap(x, r) for x, r in zip(g, rot)] + [f("diff_out_gain")] + [
        f(n) for n in ("diff_lq1", "diff_lk1", "diff_lq2", "diff_lk2")], 1)
    pos = np.arange(S)
    cm, snm = _cos_sin(pos, MROPE, 10000.0)
    cd, sd = _cos_sin(pos, DQ, 10000.0)
    cr, sr = _cos_sin(pos // GRID_W, GD // 2, 10000.0)
    cc, sc = _cos_sin(pos % GRID_W, GD // 2, 10000.0)
    one, zero = np.ones((S, MNOPE), np.float32), np.zeros((S, MNOPE), np.float32)
    mc, msn = [one, cm, cm], [zero, -snm, snm]
    gc, gs = [cr, cr, cc, cc], [-sr, sr, -sc, sc]
    out["ropec"] = np.concatenate(mc * 2 + [cd, cd] * 2 + gc * 2, 1)
    out["ropes"] = np.concatenate(msn * 2 + [-sd, sd] * 2 + gs * 2, 1)
    c2, s2 = _cos_sin(pos, ROT, 500000.0)
    out["rotc"], out["rots"] = np.concatenate([c2, c2], 1), np.concatenate([-s2, s2], 1)
    lng = np.stack([f("emb_ln_g_2"), f("ln1_g_2")[0], f("ln2_g_2")[0], f("ln1_g_2")[1], f("ln2_g_2")[1]])
    lnb = np.stack([f("emb_ln_b_2"), f("ln1_b_2")[0], f("ln2_b_2")[0], f("ln1_b_2")[1], f("ln2_b_2")[1]])
    out["lngb"] = np.concatenate([lng, lnb], 1)
    out["bgate"], out["sink"] = f("b_gate_2"), f("sw_sink_2")
    out["router"] = np.ascontiguousarray(f("moe_router_2")[0].reshape(KD, P, NE).transpose(1, 0, 2)).reshape(P, KD * NE)
    r = f("na_rpb_2")
    kw = (r.shape[3] + 1) // 2
    col = np.arange(S) % GRID_W
    row = np.arange(S) // GRID_W
    first = np.clip(col - kw // 2, 0, GRID_W - kw)[:, None]
    inside = (col[None, :] >= first) & (col[None, :] < first + kw)
    dr = row[None, :] - row[:, None] + r.shape[2] // 2
    dc = np.clip(col[None, :] - col[:, None] + kw - 1, 0, 2 * kw - 2)
    out["rpb"] = np.where(inside, r[:, :, dr, dc], np.float32(NEG))
    t = np.arange(S)
    out["band"] = np.where(np.abs(t[:, None] - t[None, :]) <= 128, 0.0, NEG).astype(np.float32)
    out["ident"] = np.eye(P, dtype=np.float32)
    out["iota"] = np.broadcast_to(t.astype(np.float32), (P, S))
    out["iota8"] = np.broadcast_to(np.arange(NE, dtype=np.float32), (P, NE))
    out["tri"] = np.triu(np.ones((P, P), np.float32), 1)
    out["ones"] = np.ones((P, P), np.float32)
    return {n: np.ascontiguousarray(v) for n, v in out.items()}


def kernel(**inputs):
    import concourse.bacc as _bacc
    from concourse.bass_utils import run_bass_kernel_spmd as _run

    arrays = _layout(inputs)
    nc = _bacc.Bacc("TRN2", target_bir_lowering=False, num_devices=1)
    A = {n: nc.dram_tensor("in_" + n, v.shape, mybir.dt.from_np(v.dtype), kind="ExternalInput").ap()
         for n, v in arrays.items()}
    A["out"] = nc.dram_tensor("out_y", (S, D), F32, kind="ExternalOutput").ap()
    build(nc, A)
    r = _run(nc, [{"in_" + n: v for n, v in arrays.items()}], core_ids=[0])
    return r.results[0]["out_y"].reshape(1, S, D)
```
